# Optimizing a Trainium2 kernel written in Bass

```python
import math
import jax, jax.numpy as jnp
from jax import lax
import numpy as np

D_MODEL = 1024
BATCH = 1
SEQ = 2048
DEPTH = 1

CHUNK = 64
D_MIX = D_MODEL
HEAD_DIM = 64
NORM_EPS = 1e-6
RWKV_WIDTH = D_MIX // 2
RWKV_HEADS = RWKV_WIDTH // HEAD_DIM
DECAY_LORA = 32
ICLR_LORA = 32
GATE_LORA = 96
RWKV_COLS = 3 * RWKV_WIDTH + DECAY_LORA + ICLR_LORA + GATE_LORA
GN_EPS = 64e-5
ATT_WIDTH = D_MIX - RWKV_WIDTH
ATT_Q_HEADS = ATT_WIDTH // HEAD_DIM
ATT_KV_HEADS = 2
ATT_GROUP = ATT_Q_HEADS // ATT_KV_HEADS
WINDOW = 128
WINDOW_CHUNKS = WINDOW // CHUNK
KEY_BAND = WINDOW_CHUNKS * CHUNK
ATT_COLS = (ATT_Q_HEADS + 2 * ATT_KV_HEADS) * HEAD_DIM
IN_COLS = RWKV_COLS + ATT_COLS
REL_BUCKETS = 32
REL_MAX_DIST = 128
NEG_INF = -1e30
N_GROUPS = 4
EXPERTS_PER_GROUP = 8
N_EXPERTS = N_GROUPS * EXPERTS_PER_GROUP
TOP_K = 2
D_EXPERT = D_MODEL // 2
ROW_BLOCK = 128

kernel_name = "hybrid_rwkv7_swa_sink_hmoe_block"

def rms_norm(x, g):
    xf = x.astype(jnp.float32)
    y = xf * lax.rsqrt(jnp.mean(jnp.square(xf), axis=-1, keepdims=True) + NORM_EPS)
    return (y * g.astype(jnp.float32)).astype(x.dtype)

def modulate(h, shift, scale):
    return h * (1 + scale[:, None, :]) + shift[:, None, :]

def t5_bucket(rel):
    half = REL_BUCKETS // 2
    exact = half // 2
    bucket = jnp.where(rel > 0, half, 0)
    n = jnp.abs(rel)
    nf = jnp.maximum(n, 1).astype(jnp.float32)
    large = exact + (jnp.log(nf / exact) / math.log(REL_MAX_DIST / exact) * (half - exact)).astype(jnp.int32)
    large = jnp.minimum(large, half - 1)
    return bucket + jnp.where(n < exact, n, large)

def wkv7_scan(r, w, k, v, a, b):
    Bb, S, H, N = r.shape

    def step(state, inp):
        r_t, w_t, k_t, v_t, a_t, b_t = inp
        sa = jnp.einsum('bhvk,bhk->bhv', state, a_t)
        state = (state * w_t[:, :, None, :] + sa[..., None] * b_t[:, :, None, :]
                 + v_t[..., None] * k_t[:, :, None, :])
        y = jnp.einsum('bhvk,bhk->bhv', state, r_t)
        return state, y

    xs = (jnp.moveaxis(r, 1, 0), jnp.moveaxis(w, 1, 0), jnp.moveaxis(k, 1, 0),
          jnp.moveaxis(v, 1, 0), jnp.moveaxis(a, 1, 0), jnp.moveaxis(b, 1, 0))
    state0 = jnp.zeros((Bb, H, N, N), jnp.float32)
    _, ys = lax.scan(step, state0, xs)
    return jnp.moveaxis(ys, 0, 1)

def rwkv7_time_mix(feat, shift_mix, w0, w2, a0, a2, g2, k_k, k_a, r_k, ln_w, ln_b):
    Bb, S, _ = feat.shape
    H, N, C = RWKV_HEADS, HEAD_DIM, RWKV_WIDTH
    prev = jnp.pad(feat, ((0, 0), (1, 0), (0, 0)))[:, :S]
    feat = feat + (prev - feat) * shift_mix
    r, k, v, w_lo, a_lo, g_lo = jnp.split(
        feat, [C, 2 * C, 3 * C, 3 * C + DECAY_LORA, 3 * C + DECAY_LORA + ICLR_LORA], axis=-1)
    w = -jax.nn.softplus(-(w0 + jnp.tanh(w_lo) @ w2)) - 0.5
    decay = jnp.exp(-jnp.exp(w.astype(jnp.float32)))
    iclr = jax.nn.sigmoid(a0 + a_lo @ a2)
    gate = jax.nn.sigmoid(g_lo) @ g2

    def heads(t):
        return t.reshape(Bb, S, H, N).astype(jnp.float32)

    kk = heads(k * k_k)
    kk = kk / jnp.maximum(jnp.linalg.norm(kk, axis=-1, keepdims=True), 1e-12)
    k = k * (1 + (iclr - 1) * k_a)
    r_h, k_h, v_h, a_h = heads(r), heads(k), heads(v), heads(iclr)
    y = wkv7_scan(r_h, heads(decay), k_h, v_h, -kk, kk * a_h)
    mu = jnp.mean(y, axis=-1, keepdims=True)
    var = jnp.mean(jnp.square(y - mu), axis=-1, keepdims=True)
    y = (y - mu) * lax.rsqrt(var + GN_EPS) * ln_w.reshape(H, N).astype(jnp.float32) \
        + ln_b.reshape(H, N).astype(jnp.float32)
    y = y + jnp.sum(r_h * k_h * r_k.astype(jnp.float32), axis=-1, keepdims=True) * v_h
    return (y.reshape(Bb, S, C) * gate).astype(feat.dtype)

def swa_sink_attention(q, k, v, q_g, k_g, sinks, rel_bias):
    Bb, S = q.shape[0], q.shape[1]
    nC = S // CHUNK
    q = rms_norm(q, q_g).astype(jnp.float32)
    k = rms_norm(k, k_g).astype(jnp.float32)
    v = v.astype(jnp.float32)
    qc = q.reshape(Bb, nC, CHUNK, ATT_KV_HEADS, ATT_GROUP, HEAD_DIM)

    def band(t):
        tc = t.reshape(Bb, nC, CHUNK, ATT_KV_HEADS, HEAD_DIM)
        tp = jnp.pad(tc, ((0, 0), (WINDOW_CHUNKS - 1, 0), (0, 0), (0, 0), (0, 0)))
        return jnp.concatenate([tp[:, j:j + nC] for j in range(WINDOW_CHUNKS)], axis=2)

    kb, vb = band(k), band(v)
    logits = jnp.einsum('bcqhgd,bckhd->bhgcqk', qc, kb) * (HEAD_DIM ** -0.5)
    i = jnp.arange(CHUNK)[:, None]
    j = jnp.arange(KEY_BAND)[None, :]
    rel = j - (WINDOW_CHUNKS - 1) * CHUNK - i
    bias = rel_bias.astype(jnp.float32)[t5_bucket(rel)]
    bias = jnp.transpose(bias, (2, 0, 1)).reshape(ATT_KV_HEADS, ATT_GROUP, 1, CHUNK, KEY_BAND)
    c_idx = jnp.arange(nC)[:, None]
    valid = (c_idx - (WINDOW_CHUNKS - 1) + (jnp.arange(KEY_BAND) // CHUNK)[None, :]) >= 0
    logits = jnp.where(valid[:, None, :], logits + bias, NEG_INF)
    sink = jnp.broadcast_to(
        sinks.astype(jnp.float32).reshape(1, ATT_KV_HEADS, ATT_GROUP, 1, 1, 1),
        logits.shape[:-1] + (1,))
    probs = jax.nn.softmax(jnp.concatenate([logits, sink], axis=-1), axis=-1)[..., :KEY_BAND]
    out = jnp.einsum('bhgcqk,bckhd->bcqhgd', probs, vb)
    return out.reshape(Bb, S, ATT_WIDTH)

def hier_moe(h, grp_w, grp_b, exp_w, exp_b, w1, w3, w2):
    Bb, S, D = h.shape
    T = Bb * S
    ht = h.reshape(T, D)
    grp_logits = (ht @ grp_w + grp_b).astype(jnp.float32)
    grp = jnp.argmax(grp_logits, axis=-1)
    grp_gate = jnp.take_along_axis(jax.nn.softmax(grp_logits, axis=-1), grp[:, None], axis=-1)[:, 0]
    exp_logits = (ht @ exp_w + exp_b).astype(jnp.float32).reshape(T, N_GROUPS, EXPERTS_PER_GROUP)
    exp_logits = jnp.take_along_axis(exp_logits, grp[:, None, None], axis=1)[:, 0]
    top_val, top_idx = lax.top_k(exp_logits, TOP_K)
    top_w = jax.nn.softmax(top_val, axis=-1) * grp_gate[:, None]
    expert = grp[:, None] * EXPERTS_PER_GROUP + top_idx

    A = T * TOP_K
    e_flat = expert.reshape(A)
    tok_flat = jnp.repeat(jnp.arange(T, dtype=jnp.int32), TOP_K)
    w_flat = top_w.reshape(A)
    order = jnp.argsort(e_flat)
    e_sorted = e_flat[order]
    counts = jnp.bincount(e_flat, length=N_EXPERTS)
    padded = (counts + ROW_BLOCK - 1) // ROW_BLOCK * ROW_BLOCK
    pad_end = jnp.cumsum(padded)
    pad_start = pad_end - padded
    start = jnp.cumsum(counts) - counts
    dest = pad_start[e_sorted] + jnp.arange(A) - start[e_sorted]
    n_blocks = -(-(A + N_EXPERTS * (ROW_BLOCK - 1)) // ROW_BLOCK)
    R = n_blocks * ROW_BLOCK
    row_tok = jnp.full((R,), T, jnp.int32).at[dest].set(tok_flat[order])
    row_w = jnp.zeros((R,), jnp.float32).at[dest].set(w_flat[order])
    block_e = jnp.minimum(
        jnp.searchsorted(pad_end, jnp.arange(n_blocks) * ROW_BLOCK, side='right'), N_EXPERTS - 1)
    x_pad = jnp.concatenate([ht, jnp.zeros((1, D), ht.dtype)], axis=0)
    xb = x_pad[row_tok].reshape(n_blocks, ROW_BLOCK, D)

    def expert_block(args):
        xblk, e = args
        return (jax.nn.silu(xblk @ w1[e]) * (xblk @ w3[e])) @ w2[e]

    yb = lax.map(expert_block, (xb, block_e)).reshape(R, D)
    out = jnp.zeros((T + 1, D), h.dtype).at[row_tok].add((yb * row_w[:, None]).astype(h.dtype))
    return out[:T].reshape(Bb, S, D)

def setup_inputs(seed: int = 0) -> dict:
    key = jax.random.key(seed)
    ks = jax.random.split(key, 32)
    L, D, C = DEPTH, D_MODEL, RWKV_WIDTH
    nrm = jax.random.normal
    f32 = jnp.float32
    return {
        "x": nrm(ks[0], (BATCH, SEQ, D), f32),
        "c": nrm(ks[1], (BATCH, D), f32),
        "ada_w": nrm(ks[2], (L, D, 6 * D), f32) * D ** -0.5,
        "ada_b": nrm(ks[3], (L, 6 * D), f32) * 0.02,
        "norm1_g": 1.0 + 0.05 * nrm(ks[4], (L, D), f32),
        "w_in": nrm(ks[5], (L, D, IN_COLS), f32) * D ** -0.5,
        "rwkv_shift_mix": jax.random.uniform(ks[6], (L, RWKV_COLS), f32),
        "rwkv_w0": jax.random.uniform(ks[7], (L, C), f32, minval=-6.0, maxval=1.0),
        "rwkv_w2": nrm(ks[8], (L, DECAY_LORA, C), f32) * 0.1,
        "rwkv_a0": nrm(ks[9], (L, C), f32) * 0.1,
        "rwkv_a2": nrm(ks[10], (L, ICLR_LORA, C), f32) * 0.5 * ICLR_LORA ** -0.5,
        "rwkv_g2": nrm(ks[11], (L, GATE_LORA, C), f32) * GATE_LORA ** -0.5,
        "rwkv_k_k": 0.85 + 0.05 * nrm(ks[12], (L, C), f32),
        "rwkv_k_a": 1.0 + 0.05 * nrm(ks[13], (L, C), f32),
        "rwkv_r_k": 0.1 * nrm(ks[14], (L, RWKV_HEADS, HEAD_DIM), f32),
        "rwkv_ln_w": 1.0 + 0.05 * nrm(ks[15], (L, C), f32),
        "rwkv_ln_b": 0.01 * nrm(ks[16], (L, C), f32),
        "q_norm_g": 1.0 + 0.05 * nrm(ks[17], (L, HEAD_DIM), f32),
        "k_norm_g": 1.0 + 0.05 * nrm(ks[18], (L, HEAD_DIM), f32),
        "attn_sinks": 0.5 * nrm(ks[19], (L, ATT_Q_HEADS), f32),
        "rel_bias": 0.5 * nrm(ks[20], (REL_BUCKETS, ATT_Q_HEADS), f32),
        "w_out": nrm(ks[21], (L, D_MIX, D), f32) * D_MIX ** -0.5,
        "norm2_g": 1.0 + 0.05 * nrm(ks[22], (L, D), f32),
        "router_grp_w": nrm(ks[23], (L, D, N_GROUPS), f32) * D ** -0.5,
        "router_grp_b": 0.01 * nrm(ks[24], (L, N_GROUPS), f32),
        "router_exp_w": nrm(ks[25], (L, D, N_EXPERTS), f32) * D ** -0.5,
        "router_exp_b": 0.01 * nrm(ks[26], (L, N_EXPERTS), f32),
        "exp_w1": nrm(ks[27], (L, N_EXPERTS, D, D_EXPERT), f32) * D ** -0.5,
        "exp_w3": nrm(ks[28], (L, N_EXPERTS, D, D_EXPERT), f32) * D ** -0.5,
        "exp_w2": nrm(ks[29], (L, N_EXPERTS, D_EXPERT, D), f32) * D_EXPERT ** -0.5,
    }

def reference(x, c, ada_w, ada_b, norm1_g, w_in, rwkv_shift_mix, rwkv_w0, rwkv_w2, rwkv_a0,
              rwkv_a2, rwkv_g2, rwkv_k_k, rwkv_k_a, rwkv_r_k, rwkv_ln_w, rwkv_ln_b, q_norm_g,
              k_norm_g, attn_sinks, rel_bias, w_out, norm2_g, router_grp_w, router_grp_b,
              router_exp_w, router_exp_b, exp_w1, exp_w3, exp_w2):
    Bb, S, _ = x.shape
    q_end = RWKV_COLS + ATT_Q_HEADS * HEAD_DIM
    k_end = q_end + ATT_KV_HEADS * HEAD_DIM
    for l in range(DEPTH):
        mod = jax.nn.silu(c) @ ada_w[l] + ada_b[l]
        sh1, sc1, gt1, sh2, sc2, gt2 = jnp.split(mod, 6, axis=-1)

        h = modulate(rms_norm(x, norm1_g[l]), sh1, sc1)
        proj = h @ w_in[l]
        y_rwkv = rwkv7_time_mix(proj[..., :RWKV_COLS], rwkv_shift_mix[l], rwkv_w0[l],
                                rwkv_w2[l], rwkv_a0[l], rwkv_a2[l], rwkv_g2[l], rwkv_k_k[l],
                                rwkv_k_a[l], rwkv_r_k[l], rwkv_ln_w[l], rwkv_ln_b[l])
        q = proj[..., RWKV_COLS:q_end].reshape(Bb, S, ATT_Q_HEADS, HEAD_DIM)
        k = proj[..., q_end:k_end].reshape(Bb, S, ATT_KV_HEADS, HEAD_DIM)
        v = proj[..., k_end:].reshape(Bb, S, ATT_KV_HEADS, HEAD_DIM)
        y_att = swa_sink_attention(q, k, v, q_norm_g[l], k_norm_g[l], attn_sinks[l],
                                   rel_bias).astype(h.dtype)
        y = jnp.concatenate([y_rwkv.astype(h.dtype), y_att], axis=-1) @ w_out[l]
        x = x + gt1[:, None, :] * y

        h2 = modulate(rms_norm(x, norm2_g[l]), sh2, sc2)
        x = x + gt2[:, None, :] * hier_moe(h2, router_grp_w[l], router_grp_b[l], router_exp_w[l],
                                           router_exp_b[l], exp_w1[l], exp_w3[l], exp_w2[l])
    return x


_drawn_inputs = setup_inputs


def setup_inputs(seed=0):
    import zlib

    import numpy as np

    out = dict(_drawn_inputs(seed))
    spreads = {}
    factors = {'rwkv_a0': 2.852,
     'rwkv_ln_b': 17.936,
     'q_norm_g': 6.086,
     'k_norm_g': 5.202,
     'attn_sinks': 64.0,
     'router_grp_b': 15.307,
     'router_exp_b': 3.917,
     'rwkv_ln_w': 2.837}
    for name, (base, spread) in spreads.items():
        noise = np.random.default_rng([zlib.crc32(name.encode()), seed]).standard_normal(out[name].shape)
        drawn = base * np.exp(spread * noise) if base else spread * noise
        out[name] = __import__('jax').numpy.asarray(drawn.astype(out[name].dtype))
    for name, factor in factors.items():
        out[name] = (out[name] * factor).astype(out[name].dtype)
    return out
```

```python
from contextlib import ExitStack

import numpy as np
import concourse.bass as bass
from concourse import mybir

F32 = mybir.dt.float32
I32 = mybir.dt.int32
U32 = mybir.dt.uint32
ALU = mybir.AluOpType
ACT = mybir.ActivationFunctionType
AX = mybir.AxisListType

D = 1024
T = 2048
P = 128
NT = T // P
KD = D // P
CHUNK = 64
HD = 64
C = 512
H = C // HD
CC = C // P
LORA_WA = 64
LORA_G = 96
RW_COLS = 3 * C + LORA_WA + LORA_G
QH, KVH = 8, 2
IN_COLS = RW_COLS + (QH + 2 * KVH) * HD
NF = 3 * CC + 2
LAMBDA = float(np.exp(-0.5))
NEG = -1e30
KEYS = 192
NG, EG, NE, FE = 4, 8, 32, 512
NR = NG + NE
NB = (2 * T + NE * (P - 1)) // P + 1
LEVELS = (1, 2, 4, 8, 16, 32)

COLS = {}
_at = 0
for _n, _w in (("c", KD), ("ada_b", 48), ("n1g", KD), ("n2g", KD), ("mix", NF), ("w0", CC), ("a0", CC),
               ("k_k", CC), ("k_a", CC), ("r_k", CC)):
    COLS[_n] = (_at, _at + _w)
    _at += _w
NCOLS = _at
ROWS = {}
_at = 0
for _n, _w in (("ln_w", C), ("ln_b", C), ("q_g", HD), ("k_g", HD), ("sinks", QH), ("rb", NR)):
    ROWS[_n] = (_at, _at + _w)
    _at += _w
NROWS = _at
CONSTS = {}
_at = 0
for _n, _w in (("ident", P), ("scan", C), ("mmask", 4 * P), ("level", len(LEVELS) * P), ("headsel", 2),
               ("before", P), ("ones", P), ("iota_e", NE), ("group_e", NE), ("block_row", NB),
               ("token", NT), ("sel8", C)):
    CONSTS[_n] = (_at, _at + _w)
    _at += _w
NCONST = _at
PK = {}
_at = 0
for _n, _w in (("AR", 2 * C), ("BT", C), ("KT", C), ("A", C), ("B", C), ("K", C), ("V", C),
               ("gate", C), ("ya", C), ("PC", 8), ("bon", 8)):
    PK[_n] = (_at, _at + _w)
    _at += _w
NPK = _at


def shape_constants():
    k = np.zeros((P, NCONST), np.float32)
    j, t = np.arange(P)[:, None], np.arange(P)[None, :]

    def put(name, a):
        a0, a1 = CONSTS[name]
        k[:a.shape[0], a0:a1] = a

    put("ident", np.eye(P))
    put("scan", np.tile((np.arange(C) % CHUNK != 0)[None, :], (P, 1)))
    same = j // CHUNK == t // CHUNK
    strict, incl = same & (j < t), same & (j <= t)
    put("mmask", np.concatenate([strict, incl, strict, incl], 1))
    put("level", np.concatenate([(j // (2 * s) == t // (2 * s)) & (j // s % 2 == 0) & (t // s % 2 == 1)
                                 for s in LEVELS], 1))
    put("headsel", (np.arange(P)[:, None] // HD) == np.arange(2)[None, :])
    put("before", j < t)
    put("ones", np.ones((P, P)))
    put("iota_e", np.tile(np.arange(NE)[None], (P, 1)))
    put("group_e", np.tile(np.arange(NE)[None] // EG, (P, 1)))
    put("block_row", np.tile(P * np.arange(NB)[None], (P, 1)))
    put("token", np.arange(P)[:, None] + P * np.arange(NT)[None])
    ch = np.arange(C)
    put("sel8", (ch[None, :] // HD) == np.arange(8)[:, None])
    rel = np.arange(2 * CHUNK)[:, None] - CHUNK - np.arange(CHUNK)[None, :]
    n = np.abs(rel)
    nf = np.maximum(n, 1).astype(np.float32)
    large = 8 + (np.log(nf / np.float32(8)) / np.float32(np.log(16.0)) * np.float32(8)).astype(np.int32)
    bucket = np.where(rel > 0, 16, 0) + np.where(n < 8, n, np.minimum(large, 15))
    onehot = (np.arange(32)[:, None, None] == bucket[None]).astype(np.float32)
    return k, onehot.reshape(32, 2 * CHUNK * CHUNK)


USES1 = {"A0": ("r", "v", "q"), "A1": ("k", "lora", "kv"),
         "T0": ("xT", "qT", "tokA", "tokK", "P0", "P1"), "T1": ("xT", "kT", "tokB", "tokV", "P0", "P1"),
         "C0": ("zw", "nbc", "L0", "L1"), "C1": ("za", "L0", "L1"),
         "C2": ("gate",), "C3": ("ssn", "nT", "bon")}
BANK1 = {b: i for i, b in enumerate(USES1)}
IN_GROUPS = {"r": ("A0", 0), "k": ("A1", 1), "v": ("A0", 2), "lora": ("A1", 3)}


class Sync:

    def __init__(self, nc, ctx):
        self.nc, self.ctx, self.sems = nc, ctx, {}

    def __getitem__(self, name):
        if name not in self.sems:
            self.sems[name] = self.ctx.enter_context(self.nc.semaphore("s_" + name))
        return self.sems[name]

    def wait(self, eng, name, value):
        if isinstance(value, int) and value <= 0:
            return
        eng.wait_ge(self[name], value)


class Banks:

    def __init__(self, sync, prefix, uses, nt, ahead=()):
        self.sync, self.prefix, self.uses, self.nt, self.ahead = sync, prefix, uses, nt, ahead

    def _nth(self, bank, use, t):
        uses = self.uses[bank]
        early = [u for u in uses if u in self.ahead]
        at = uses.index(use)
        if use in early:
            return early.index(use) if isinstance(t, int) and t == 0 else len(early) + len(uses) * (t - 1) + at
        if isinstance(t, int) and t == self.nt - 1:
            at -= sum(u in early for u in uses[:at])
        return len(early) + len(uses) * t + at

    def wait_free(self, pe, bank, use, t):
        self.sync.wait(pe, f"{self.prefix}{bank}_free", self._nth(bank, use, t))

    def full(self, ins, bank):
        ins.then_inc(self.sync[f"{self.prefix}{bank}_full"], 1)

    def wait_full(self, eng, bank, use, t):
        if isinstance(t, int) and t < 0:
            return
        self.sync.wait(eng, f"{self.prefix}{bank}_full", self._nth(bank, use, t) + 1)

    def free(self, ins, bank):
        ins.then_inc(self.sync[f"{self.prefix}{bank}_free"], 1)

    def wait_read(self, eng, bank, use, t):
        if isinstance(t, int) and t < 0:
            return
        self.sync.wait(eng, f"{self.prefix}{bank}_free", self._nth(bank, use, t) + 1)


class Arena:

    def __init__(self, tensor, at=0):
        self.tensor, self.at = tensor, at

    def take(self, width):
        a = self.tensor[:, self.at:self.at + width]
        self.at += width
        return a


def split(ap, a):
    return ap.rearrange("p (a b) -> p a b", a=a)


def per_channel(col, n):
    p, k = col.shape
    return col.unsqueeze(2).to_broadcast([p, k, n])


def setup(nc, S, ps, V, ins, dram):
    ada = V["ada_slots"]
    pieces = [0, 1, 2, 3, 6, 7, 8, 9, 4, 5, 10, 11]
    ada_v = ins["ada_w"].rearrange("(k p) n -> p k n", p=P)
    col, row = V["col"], V["row"]
    with nc.Block() as block:
        @block.sync
        def _(sp):
            sp.dma_start(V["cols"], ins["cols"]).then_inc(S["params"], 16)
            sp.dma_start(V["rows"], ins["rows"].to_broadcast([P, NROWS])).then_inc(S["params"], 16)
            sp.dma_start(V["consts"], ins["consts"]).then_inc(S["params"], 16)
            sp.dma_start(V["onehot"][0:32, :], ins["onehot"]).then_inc(S["params"], 16)
            sp.dma_start(V["rel_bias"][0:32, :], ins["rel_bias"]).then_inc(S["params"], 16)
            sp.dma_start(V["gate_b"], ins["gate_b"].to_broadcast([P, 2 * D])).then_inc(S["params"], 16)
            for n, piece in enumerate(pieces):
                if n >= 2:
                    sp.wait_ge(S["ada_used"], n - 1)
                sp.dma_start(ada[n % 2], ada_v[:, :, 512 * piece:512 * piece + 512]).then_inc(S[f"ada_in{n % 2}"], 16)
            sp.wait_ge(S["rows_done"], 4)
            sp.dma_start(V["w_in"], ins["w_in"].rearrange("(k p) n -> p k n", p=P)).then_inc(S["w_in"], 16)
            sp.dma_start(V["w2"][0:32, :], ins["w2"]).then_inc(S["params"], 16)
            sp.dma_start(V["w2"][32:64, :], ins["a2"]).then_inc(S["params"], 16)
            sp.dma_start(V["g2"][0:LORA_G, :], ins["g2"]).then_inc(S["params"], 16)
            sp.dma_start(dram["gates"], V["gt"]).then_inc(S["gates_out"], 16)
            sp.wait_ge(S["gates_out"], 16)
            sp.wait_ge(S["w_in"], 16)
            sp.wait_ge(S["params"], 144)

        @block.scalar
        def _(act):
            act.wait_ge(S["params"], 96)
            act.activation(V["csig"], col("c"), ACT.Sigmoid).then_inc(S["csig"], 1)

        @block.tensor
        def _(pe):
            pe.wait_ge(S["params"], 96)
            for j in range(2 * CHUNK):
                for half in range(2):
                    mm = pe.matmul(ps[j // 64][64 * half:64 * half + 64, 8 * (j % 64):8 * (j % 64) + 8],
                                   V["onehot"][0:32, 64 * j:64 * j + 64], V["rel_bias"][0:32, :],
                                   start=True, stop=True)
            mm.then_inc(S["bias_mm"], 1)
            pe.wait_ge(S["cs"], 2)
            for n, piece in enumerate(pieces):
                pe.wait_ge(S[f"ada_in{n % 2}"], 16 * (n // 2 + 1))
                if n < 8:
                    for m in range(4):
                        for k in range(KD):
                            mm = pe.matmul(ps[2][:, 4 * n + m:4 * n + m + 1], ada[n % 2][:, k, 128 * m:128 * m + 128],
                                           V["cs"][:, k:k + 1], start=(k == 0), stop=(k == KD - 1))
                else:
                    for k in range(KD):
                        mm = pe.matmul(ps[4 + n - 8][:, :], V["cs_rows"][:, k, :], ada[n % 2][:, k, :],
                                       start=(k == 0), stop=(k == KD - 1))
                mm.then_inc(S["ada_used"], 1)

        @block.gpsimd
        def _(pool):
            pool.memset(V["bias"], NEG).then_inc(S["bias_fill"], 1)
            for name in ("raw", "qkv1", "Pm", "kT"):
                pool.memset(V[name], 0.0)
            pool.memset(V["minus_half"], -0.5)
            pool.memset(V["Pb"], 1.0)
            pool.memset(V["S"], 0.0)

        @block.vector
        def _(dve):
            dve.wait_ge(S["csig"], 1)
            dve.tensor_tensor(V["cs"], V["csig"], col("c"), ALU.mult).then_inc(S["cs"], 1)
            dve.drain()
            dve.tensor_copy(V["cs_rows"], per_channel(V["cs"], P)).then_inc(S["cs"], 1)
            dve.wait_ge(S["bias_fill"], 1)
            dve.wait_ge(S["bias_mm"], 1)
            bias = V["bias_v"]
            for j0 in range(2):
                b = ps[j0][:, :].rearrange("p (j h) -> p h j", h=QH)
                if j0 == 0:
                    dve.tensor_copy(V["bias_first"][0:64], b[0:64])
                else:
                    dve.tensor_copy(bias[0:64, :, 64:128], b[0:64])
                dve.tensor_copy(bias[64:128, :, 64 + 64 * j0:128 + 64 * j0], b[64:128])
            dve.tensor_tensor(V["rksel"], per_channel(col("r_k"), 2),
                              V["k"]("headsel").unsqueeze(1).to_broadcast([P, CC, 2]), ALU.mult)
            dve.tensor_scalar(V["omka"], col("k_a"), -1.0, 1.0, ALU.mult, ALU.add)
            dve.wait_ge(S["ada_used"], 8)
            ab = COLS["ada_b"][0]
            for i, (name, b0) in enumerate((("b1", 0), ("s1", 8), ("b2", 24), ("s2", 32))):
                dve.tensor_tensor(V[name], ps[2][:, 8 * i:8 * i + 8], V["cols"][:, ab + b0:ab + b0 + 8], ALU.add)
            dve.drain()
            for s, g in (("s1", "n1g"), ("s2", "n2g")):
                dve.scalar_tensor_tensor(V[s], V[s], 1.0, col(g), ALU.add, ALU.mult)
            for n in range(4):
                dve.wait_ge(S["ada_used"], 9 + n)
                cols = slice(512 * n, 512 * n + 512)
                dve.tensor_tensor(V["gt"][:, cols], ps[4 + n][:, :], V["gate_b"][:, cols], ALU.add).then_inc(S["rows_done"], 1)


def pass1(nc, S, ps, V, dram, nt):
    B = Banks(S, "a", USES1, nt, ahead=("xT", "r", "k", "v", "lora", "q", "kv"))
    bank = {b: ps[i] for b, i in BANK1.items()}
    k, col, row, pk = V["k"], V["col"], V["row"], V["pk"]
    ident = k("ident")
    heads4 = lambda h: (64 * (h % 2), h // 2)

    ORDER = (("norm", 1), ("att1", 0), ("lora1", 0), ("xT", 1), ("in_r", 1), ("ew1", 0), ("in_k", 1), ("ev_r", 1),
             ("ew2", 0), ("att2", 0), ("in_v", 1), ("ev_k", 1), ("ew3", 0), ("att3_0", 0), ("in_lora", 1),
             ("ev_v", 1), ("tok", 0), ("att4_0", 0), ("att3_1", 0), ("in_q", 1), ("ev_lora", 1), ("att4_1", 0),
             ("in_kv", 1), ("ev_q", 1), ("att5", 0), ("ev_kv", 1))

    def run(eng, steps):
        def tile(t, parity, front=True, back=True):
            for name, ahead in ORDER:
                if (front if ahead else back) and name in steps:
                    steps[name](t + ahead, (parity + ahead) % 2)

        tile(-1, 1, back=False)
        tile(0, 0)
        tile(1, 1)
        if nt > 4:
            with eng.Fori(1, nt // 2 - 1) as u:
                tile(2 * u, 0)
                tile(2 * u + 1, 1)
        tile(nt - 2, 0)
        tile(nt - 1, 1, front=False)

    with nc.Block() as block:
        @block.sync
        def _(sp):
            def load_x(n, b):
                B.wait_full(sp, "T1", "xT", n - 1)
                sp.dma_start(V["x"], dram["x"][bass.ds(n * P, P), :]).then_inc(S["x"], 16)

            def store(t, b):
                S.wait(sp, "ya", t + 1)
                B.wait_read(sp, "T0", "tokK", t)
                sp.dma_start(dram["mid"][bass.ds(t, 1)].rearrange("a p n -> (a p) n"), V["pk_all"]).then_inc(S["stored"], 16)

            run(sp, {"norm": load_x, "att5": store})
            sp.wait_ge(S["stored"], 16 * nt)

        @block.tensor
        def _(pe):
            def xT(n, b):
                S.wait(pe, "xn", n + 1)
                for half, name in enumerate(("T0", "T1")):
                    B.wait_free(pe, name, "xT", n)
                    for i in range(4):
                        c = 4 * half + i
                        mm = pe.transpose(bank[name][:, P * i:P * i + P], V["x"][:, P * c:P * c + P], ident)
                    B.full(mm, name)

            def in_group(g):
                name, index = IN_GROUPS[g]

                def go(n, b):
                    B.wait_read(pe, "T1", "xT", n)
                    B.wait_free(pe, name, g, n)
                    parts = [(P * c, P, C * index + P * c) for c in range(4)]
                    if g == "lora":
                        parts = [(0, LORA_WA, 3 * C), (P, LORA_G, 3 * C + LORA_WA)]
                    for at, m, w0 in parts:
                        for kk in range(KD):
                            mm = pe.matmul(bank[name][0:m, at:at + P], V["w_in"][:, kk, w0:w0 + m], V["hT"][:, kk, :],
                                           start=(kk == 0), stop=(kk == KD - 1))
                    B.full(mm, name)
                return go

            def in_tok(g, name, w0, w):
                def go(n, b):
                    B.wait_free(pe, name, g, n)
                    for kk in range(KD):
                        mm = pe.matmul(bank[name][:, 0:w], V["hT"][:, kk, :], V["w_in"][:, kk, w0:w0 + w],
                                       start=(kk == 0), stop=(kk == KD - 1))
                    B.full(mm, name)
                return go

            def lora1(t, b):
                S.wait(pe, "lora_in", t + 1)
                B.wait_free(pe, "C0", "zw", t)
                for c in range(CC):
                    mm = pe.matmul(bank["C0"][:, P * c:P * c + P], V["w2"][0:32, P * c:P * c + P], V["tw"][0:32, :],
                                   start=True, stop=True)
                B.full(mm, "C0")
                B.wait_free(pe, "C1", "za", t)
                for c in range(CC):
                    mm = pe.matmul(bank["C1"][:, P * c:P * c + P], V["w2"][32:64, P * c:P * c + P],
                                   V["f"][b][32:64, 3 * CC, :], start=True, stop=True)
                B.full(mm, "C1")
                B.wait_free(pe, "C2", "gate", t)
                S.wait(pe, "ya", t)
                mm = pe.matmul(bank["C2"][:, :], V["sg"][0:LORA_G, :], V["g2"][0:LORA_G, :], start=True, stop=True)
                B.full(mm, "C2")

            def ew1(t, b):
                S.wait(pe, "sq", t + 1)
                B.wait_free(pe, "C3", "ssn", t)
                for c in range(CC):
                    mm = pe.matmul(bank["C3"][:, 2 * c:2 * c + 2], V["sq"][:, P * c:P * c + P], k("headsel"),
                                   start=True, stop=True)
                B.full(mm, "C3")

            def ew2(t, b):
                S.wait(pe, "ninv", t + 1)
                B.wait_free(pe, "C3", "nT", t)
                B.full(pe.transpose(bank["C3"][0:8, 0:P], V["ninv"], ident), "C3")
                B.wait_read(pe, "C3", "nT", t)
                B.wait_free(pe, "C0", "nbc", t)
                for c in range(CC):
                    mm = pe.matmul(bank["C0"][:, P * c:P * c + P], k("sel8")[0:8, P * c:P * c + P], V["nT"][0:8, :],
                                   start=True, stop=True)
                B.full(mm, "C0")

            def tok(t, b):
                S.wait(pe, "ew3", t + 1)
                src = {"tokA": lambda c: pk["AR_v"][:, c, 0, :], "tokB": lambda c: split(pk["BT"], 4)[:, c, :],
                       "tokK": lambda c: split(pk["KT"], 4)[:, c, :], "tokV": lambda c: V["f"][b][:, 2 * CC + c, :]}
                for use, name in (("tokA", "T0"), ("tokB", "T1"), ("tokK", "T0"), ("tokV", "T1")):
                    B.wait_free(pe, name, use, t)
                    for c in range(CC):
                        mm = pe.transpose(bank[name][:, P * c:P * c + P], src[use](c), ident)
                    B.full(mm, name)
                S.wait(pe, "rk", t + 1)
                B.wait_free(pe, "C3", "bon", t)
                for c in range(CC):
                    mm = pe.matmul(bank["C3"][:, 2 * c:2 * c + 2], V["rk"][:, P * c:P * c + P], V["rksel"][:, c, :],
                                   start=True, stop=True)
                B.full(mm, "C3")

            def att2(t, b):
                S.wait(pe, "qn", t + 1)
                for name, use, n, base in (("T0", "qT", 4, 0), ("T1", "kT", 2, C)):
                    B.wait_free(pe, name, use, t)
                    for i in range(n):
                        mm = pe.transpose(bank[name][:, P * i:P * i + P], V["qn"][:, base + P * i:base + P * i + P], ident)
                    B.full(mm, name)

            def att3(g):
                def go(t, b):
                    B.wait_read(pe, "T0", "qT", t)
                    B.wait_read(pe, "T1", "kT", t)
                    for i in range(4):
                        h = 4 * g + i
                        hp, c = heads4(h)
                        name = f"C{i % 2}"
                        if i < 2:
                            B.wait_free(pe, name, f"L{g}", t)
                        mm = pe.matmul(bank[name][:, KEYS * (i // 2):KEYS * (i // 2) + KEYS],
                                       V["qT"][hp:hp + 64, P * c:P * c + P], V["kT_v"][hp:hp + 64, g, :],
                                       start=True, stop=True)
                        if i >= 2:
                            B.full(mm, name)
                return go

            def att4(g):
                def go(t, b):
                    S.wait(pe, "probs", 2 * t + g + 1)
                    for half, name in enumerate(("T0", "T1")):
                        B.wait_free(pe, name, f"P{g}", t)
                        for i in range(2):
                            for part in range(2):
                                mm = pe.transpose(bank[name][:, 256 * i + P * part:256 * i + P * part + P],
                                                  V["Pm_v"][:, 2 * half + i, P * part:P * part + P], ident)
                        B.full(mm, name)
                    B.wait_read(pe, "C2", "gate", t)
                    for i in range(4):
                        h = 4 * g + i
                        B.wait_read(pe, f"T{i // 2}", f"P{g}", t)
                        for part in range(2):
                            v = V["qkv"][b if part else 1 - b][:, 640 + 64 * g:704 + 64 * g]
                            mm = pe.matmul(bank["C2"][:, 64 * h:64 * h + 64], V["PT"][:, i, P * part:P * part + P], v,
                                           start=(part == 0), stop=(part == 1))
                    mm.then_inc(S["pv"], 1)
                return go

            run(pe, {"xT": xT, "in_r": in_group("r"), "in_k": in_group("k"), "in_v": in_group("v"),
                     "in_lora": in_group("lora"), "in_q": in_tok("q", "A0", RW_COLS, C),
                     "in_kv": in_tok("kv", "A1", RW_COLS + C, 2 * P), "lora1": lora1, "ew1": ew1, "ew2": ew2,
                     "tok": tok, "att2": att2, "att3_0": att3(0), "att3_1": att3(1),
                     "att4_0": att4(0), "att4_1": att4(1)})

        @block.scalar
        def _(act):
            def norm(n, b):
                S.wait(act, "x", 16 * n + 16)
                act.activation(V["junk"], V["x"], ACT.Square, accum_out=V["ssx"]).then_inc(S["ssx"], 1)

            def xT(n, b):
                for half, name in enumerate(("T0", "T1")):
                    B.wait_full(act, name, "xT", n)
                    if half == 0:
                        B.wait_full(act, "A1", "kv", n - 1)
                    for i in range(4):
                        c = 4 * half + i
                        a = act.activation(V["hT"][:, c, :], bank[name][:, P * i:P * i + P], ACT.Identity,
                                           scale=V["s1"][:, c:c + 1], bias=V["b1"][:, c:c + 1])
                        if i == 3:
                            B.free(a, name)

            def ev(g):
                name, index = IN_GROUPS[g]

                def go(n, b):
                    B.wait_full(act, name, g, n)
                    S.wait(act, "feat", 4 * (n - 1) + index + 1)
                    S.wait(act, "hist", 4 * (n - 1) + index + 1)
                    if g == "lora":
                        act.activation(V["raw_v"][0:LORA_WA, 12, 1:P + 1], bank[name][0:LORA_WA, 0:P], ACT.Copy)
                        a = act.activation(V["raw_v"][0:LORA_G, 13, 1:P + 1], bank[name][0:LORA_G, P:2 * P], ACT.Copy)
                    else:
                        a = act.activation(V["raw_v"][:, 4 * index:4 * index + 4, 1:P + 1],
                                           split(bank[name][:, :], 4), ACT.Copy)
                    B.free(a, name)
                return go

            def ev_q(n, b):
                B.wait_full(act, "A0", "q", n)
                B.free(act.activation(V["qkv"][b][:, 0:C], bank["A0"][:, :], ACT.Copy), "A0")

            def ev_kv(n, b):
                B.wait_full(act, "A1", "kv", n)
                S.wait(act, "pv", 2 * n)
                B.free(act.activation(V["qkv"][b][:, C:768], bank["A1"][:, 0:2 * P], ACT.Copy), "A1")

            def lora1(t, b):
                S.wait(act, "feat", 4 * t + 4)
                B.wait_full(act, "C2", "gate", t - 1)
                act.activation(V["tw"][0:32, :], V["f"][b][0:32, 12, :], ACT.Tanh)
                act.activation(V["sg"][0:LORA_G, :], V["f"][b][0:LORA_G, 13, :], ACT.Sigmoid).then_inc(S["lora_in"], 1)

            def ew1(t, b):
                S.wait(act, "ew3", t)
                for name, use, out, bias in (("C0", "zw", "sw", "w0"), ("C1", "za", "sa", "a0")):
                    B.wait_full(act, name, use, t)
                    for c in range(CC):
                        a = act.activation(V[out][:, P * c:P * c + P], bank[name][:, P * c:P * c + P], ACT.Sigmoid,
                                           bias=col(bias)[:, c:c + 1])
                    B.free(a, name)
                S.wait(act, "stored", 16 * t)
                B.wait_full(act, "C2", "gate", t)
                B.free(act.activation(pk["gate"], bank["C2"][:, :], ACT.Copy), "C2")
                S.wait(act, "kkr", t + 1)
                B.wait_full(act, "C3", "bon", t - 1)
                act.activation(V["sq"], V["kk"], ACT.Square).then_inc(S["sq"], 1)

            def ew2(t, b):
                S.wait(act, "cum", t + 1)
                act.activation(V["Pb_v"][:, :, 1:65], split(V["cum"], 8), ACT.Exp, scale=-LAMBDA)
                act.activation(V["Pinv"], V["cum"], ACT.Exp, scale=LAMBDA).then_inc(S["decay"], 1)

            def tok(t, b):
                for use in ("tokA", "tokK"):
                    B.wait_full(act, "T0", use, t)
                    B.free(act.activation(pk[use[3]], bank["T0"][:, :], ACT.Copy), "T0")

            def att1(t, b):
                act.drain()
                B.wait_read(act, "A1", "kv", t)
                act.activation(V["sqk"], V["qkv"][b][:, 0:640], ACT.Square).then_inc(S["sqk"], 1)

            def att2(t, b):
                B.wait_full(act, "T0", "qT", t)
                B.free(act.activation(V["qT"], bank["T0"][:, :], ACT.Copy), "T0")
                B.wait_full(act, "T1", "kT", t)
                B.free(act.activation(V["kT_v"][:, :, 64:KEYS], split(bank["T1"][:, 0:256], 2), ACT.Copy), "T1")

            def att3(g):
                def go(t, b):
                    S.wait(act, "negm", 2 * t + g + 1)
                    B.wait_full(act, "T1", "P1" if g == 0 else "P0", t - 1 + g)
                    for i in range(4):
                        h = 4 * g + i
                        act.activation(V["Pm_v"][:, i, 64:256], V["L"][:, i, :], ACT.Exp,
                                       bias=V["negm"][:, h:h + 1], accum_out=V["sm"][:, h:h + 1])
                    act.activation(V["es"][:, 4 * g:4 * g + 4], V["sd"][:, 4 * g:4 * g + 4], ACT.Exp).then_inc(S["probs"], 1)
                    if g == 1:
                        act.activation(V["kT_v"][:, :, 0:64], V["kT_v"][:, :, 128:192], ACT.Copy)
                        act.drain()
                return go

            def att4(g):
                def go(t, b):
                    B.wait_full(act, "T0", f"P{g}", t)
                    S.wait(act, "pv", 2 * t + g)
                    B.free(act.activation(V["PT"][:, 0:2, :], split(bank["T0"][:, :], 2), ACT.Copy), "T0")
                return go

            run(act, {"norm": norm, "xT": xT, "ev_r": ev("r"), "ev_k": ev("k"), "ev_v": ev("v"), "ev_lora": ev("lora"),
                      "ev_q": ev_q, "ev_kv": ev_kv, "lora1": lora1, "ew1": ew1, "ew2": ew2, "tok": tok, "att1": att1,
                      "att2": att2, "att3_0": att3(0), "att3_1": att3(1), "att4_0": att4(0), "att4_1": att4(1)})

        @block.gpsimd
        def _(pool):
            def norm(n, b):
                S.wait(pool, "msx", n + 1)
                pool.tensor_tensor(V["rsx"], V["msx"], V["minus_half"][:, 0:1], ALU.pow).then_inc(S["rsx"], 1)

            def ev(g):
                name, index = IN_GROUPS[g]
                m = LORA_G if g == "lora" else P
                c0, c1 = (12, 14) if g == "lora" else (4 * index, 4 * index + 4)

                def go(n, b):
                    B.wait_read(pool, name, g, n)
                    S.wait(pool, "feat", 4 * n + index)
                    raw = V["raw_v"]
                    pool.tensor_tensor(V["delta"][0:m, 0:c1 - c0, :], raw[0:m, c0:c1, 0:P], raw[0:m, c0:c1, 1:P + 1],
                                       ALU.subtract).then_inc(S["delta"], 1)
                    pool.drain()
                    pool.tensor_copy(raw[0:m, c0:c1, 0:1], raw[0:m, c0:c1, P:P + 1]).then_inc(S["hist"], 1)
                return go

            def att1(t, b):
                S.wait(pool, "ms10", t + 1)
                pool.tensor_tensor(V["rs10"], V["ms10"], V["minus_half"], ALU.pow).then_inc(S["rs10"], 1)

            def ew1(t, b):
                B.wait_read(pool, "C3", "ssn", t)
                pool.tensor_tensor(V["ninv"], V["ssm"], V["minus_half"][:, 0:8], ALU.pow).then_inc(S["ninv"], 1)

            def ew3(t, b):
                S.wait(pool, "kp", t + 1)
                B.wait_full(pool, "C3", "bon", t - 1)
                pool.tensor_tensor(V["rk"], V["f"][b][:, 0:4, :].rearrange("p c n -> p (c n)"), V["kp"],
                                   ALU.mult).then_inc(S["rk"], 1)

            run(pool, {"norm": norm, "ev_r": ev("r"), "ev_k": ev("k"), "ev_v": ev("v"), "ev_lora": ev("lora"),
                       "att1": att1, "ew1": ew1, "ew3": ew3})

        @block.vector
        def _(dve):
            def norm(n, b):
                S.wait(dve, "ssx", n + 1)
                dve.tensor_scalar(V["msx"], V["ssx"], 1.0 / D, 1e-6, ALU.mult, ALU.add).then_inc(S["msx"], 1)
                S.wait(dve, "rsx", n + 1)
                dve.tensor_scalar(V["x"], V["x"], V["rsx"][:, 0:1], None, ALU.mult).then_inc(S["xn"], 1)

            def ev(g):
                name, index = IN_GROUPS[g]
                m = LORA_G if g == "lora" else P
                c0, c1 = (12, 14) if g == "lora" else (4 * index, 4 * index + 4)

                def go(n, b):
                    S.wait(dve, "delta", 4 * n + index + 1)
                    for c in range(c0, c1):
                        i = dve.scalar_tensor_tensor(V["f"][b][0:m, c, :], V["delta"][0:m, c - c0, :],
                                                     col("mix")[0:m, c:c + 1], V["raw_v"][0:m, c, 1:P + 1],
                                                     ALU.mult, ALU.add)
                    i.then_inc(S["feat"], 1)
                return go

            def att1(t, b):
                S.wait(dve, "sqk", t + 1)
                dve.tensor_reduce(V["ms10"], split(V["sqk"], 10), AX.X, ALU.add)
                dve.drain()
                dve.tensor_scalar(V["ms10"], V["ms10"], 1.0 / HD, 1e-6, ALU.mult, ALU.add).then_inc(S["ms10"], 1)
                S.wait(dve, "rs10", t + 1)
                B.wait_full(dve, "T1", "kT", t - 1)
                qk = V["qkv"][b]
                qn = split(V["qn"][:, 0:C], QH)
                kn = V["qn"][:, C:C + 256].rearrange("p (a e n) -> p a e n", a=2, e=2)
                dve.tensor_tensor(qn, split(qk[:, 0:C], QH), per_channel(V["rs10"][:, 0:8], HD), ALU.mult)
                dve.tensor_tensor(split(V["kn"], 2), split(qk[:, C:C + P], 2), per_channel(V["rs10"][:, 8:10], HD), ALU.mult)
                dve.drain()
                dve.tensor_tensor(qn, qn, row("q_g").unsqueeze(1).to_broadcast([P, QH, HD]), ALU.mult)
                kg = row("k_g").unsqueeze(1).to_broadcast([P, 2, HD])
                dve.tensor_tensor(kn[:, :, 0, :], split(V["kn"], 2), kg, ALU.mult)
                dve.tensor_tensor(kn[:, :, 1, :], split(V["kn"], 2), kg, ALU.mult).then_inc(S["qn"], 1)

            def ew1(t, b):
                fk = V["f"][b][:, CC:2 * CC, :]
                dve.tensor_tensor(split(V["kk"], CC), fk, per_channel(col("k_k"), P), ALU.mult).then_inc(S["kkr"], 1)
                B.wait_full(dve, "C3", "ssn", t)
                B.free(dve.tensor_scalar(V["ssm"], bank["C3"][:, 0:8], 1e-24, None, ALU.max), "C3")

            def ew2(t, b):
                B.wait_read(dve, "C0", "zw", t)
                dve.tensor_tensor_scan(V["cum"], k("scan"), V["sw"], 0.0, ALU.mult, ALU.add).then_inc(S["cum"], 1)
                B.wait_full(dve, "C3", "nT", t)
                B.free(dve.tensor_copy(V["nT"][0:8, :], bank["C3"][0:8, 0:P]), "C3")
                B.wait_full(dve, "C0", "nbc", t)
                S.wait(dve, "sq", t + 1)
                B.free(dve.scalar_tensor_tensor(V["kk"], V["kk"], -1.0, bank["C0"][:, :], ALU.mult, ALU.mult), "C0")

            def ew3(t, b):
                f = V["f"][b]
                B.wait_read(dve, "C1", "za", t)
                for c in range(CC):
                    dve.tensor_scalar(V["kp"][:, P * c:P * c + P], V["sa"][:, P * c:P * c + P], col("k_a")[:, c:c + 1],
                                      V["omka"][:, c:c + 1], ALU.mult, ALU.add)
                dve.drain()
                S.wait(dve, "stored", 16 * t)
                dve.scalar_tensor_tensor(V["bb"], V["kk"], -1.0, V["sa"], ALU.mult, ALU.mult)
                dve.tensor_tensor(split(V["kp"], CC), split(V["kp"], CC), f[:, CC:2 * CC, :], ALU.mult).then_inc(S["kp"], 1)
                S.wait(dve, "decay", t + 1)
                Pb, AR = V["Pb_v"], pk["AR_v"]
                q4 = lambda ap: ap.rearrange("p c (q n) -> p c q n", q=2)
                dve.tensor_tensor(q4(AR[:, :, 0, :]), V["kk"].rearrange("p (c q n) -> p c q n", c=CC, q=2),
                                  Pb[:, :, 0:64].rearrange("p (c q) n -> p c q n", q=2), ALU.mult)
                dve.tensor_tensor(q4(AR[:, :, 1, :]), q4(f[:, 0:CC, :]),
                                  Pb[:, :, 1:65].rearrange("p (c q) n -> p c q n", q=2), ALU.mult)
                dve.drain()
                dve.tensor_tensor(pk["BT"], V["bb"], V["Pinv"], ALU.mult)
                dve.tensor_tensor(pk["KT"], V["kp"], V["Pinv"], ALU.mult)
                dve.tensor_copy(pk["PC"].unsqueeze(2), Pb[:, :, 64:65]).then_inc(S["ew3"], 1)

            def tok(t, b):
                for use in ("tokB", "tokV"):
                    B.wait_full(dve, "T1", use, t)
                    B.free(dve.tensor_copy(pk[use[3]], bank["T1"][:, :]), "T1")
                B.wait_full(dve, "C3", "bon", t)
                B.free(dve.tensor_copy(pk["bon"], bank["C3"][:, 0:8]), "C3")

            def att3(g):
                def go(t, b):
                    S.wait(dve, "probs", 2 * t + g)
                    for i in (0, 1):
                        name = f"C{i}"
                        B.wait_full(dve, name, f"L{g}", t)
                        B.free(dve.scalar_tensor_tensor(V["L"][:, i:4:2, :], split(bank[name][:, 0:2 * KEYS], 2),
                                                        HD ** -0.5, V["bias_v"][:, 4 * g + i:4 * g + 4:2, :],
                                                        ALU.mult, ALU.add), name)
                    g4 = slice(4 * g, 4 * g + 4)
                    dve.drain()
                    dve.tensor_reduce(V["negm"][:, g4], V["L"], AX.X, ALU.max)
                    dve.drain()
                    dve.tensor_tensor(V["negm"][:, g4], V["negm"][:, g4], row("sinks")[:, g4], ALU.max)
                    dve.drain()
                    dve.tensor_tensor(V["sd"][:, g4], row("sinks")[:, g4], V["negm"][:, g4], ALU.subtract)
                    dve.drain()
                    dve.tensor_scalar(V["negm"][:, g4], V["negm"][:, g4], -1.0, None, ALU.mult).then_inc(S["negm"], 1)
                    if g == 1 and isinstance(t, int) and t == 0:
                        dve.tensor_copy(V["bias_v"][0:64, :, 0:64], V["bias_first"][0:64])
                return go

            def att4(g):
                def go(t, b):
                    B.wait_full(dve, "T1", f"P{g}", t)
                    S.wait(dve, "pv", 2 * t + g)
                    B.free(dve.tensor_copy(V["PT"][:, 2:4, :], split(bank["T1"][:, :], 2)), "T1")
                return go

            def att5(t, b):
                S.wait(dve, "probs", 2 * t + 2)
                dve.tensor_tensor(V["den"], V["sm"], V["es"], ALU.add)
                dve.drain()
                dve.reciprocal(V["den"], V["den"])
                dve.drain()
                S.wait(dve, "pv", 2 * t + 2)
                dve.tensor_tensor(split(pk["ya"], QH), split(bank["C2"][:, :], QH), per_channel(V["den"], HD), ALU.mult).then_inc(S["ya"], 1)

            run(dve, {"norm": norm, "ev_r": ev("r"), "ev_k": ev("k"), "ev_v": ev("v"), "ev_lora": ev("lora"),
                      "att1": att1, "ew1": ew1, "ew2": ew2, "ew3": ew3, "tok": tok, "att3_0": att3(0),
                      "att3_1": att3(1), "att4_0": att4(0), "att4_1": att4(1), "att5": att5})


def views(nc, ctx):
    total = 53200
    arena = ctx.enter_context(nc.sbuf_tensor("arena", [P, total], F32))
    V = {}
    a = Arena(arena)
    for name, w in (("consts", NCONST), ("cols", NCOLS), ("rows", NROWS)):
        V[name] = a.take(w)
    V["k"] = lambda n: V["consts"][:, CONSTS[n][0]:CONSTS[n][1]]
    V["col"] = lambda n: V["cols"][:, COLS[n][0]:COLS[n][1]]
    V["row"] = lambda n: V["rows"][:, ROWS[n][0]:ROWS[n][1]]
    for name in ("s1", "b1", "s2", "b2"):
        V[name] = a.take(KD)
    V["omka"] = a.take(CC)
    V["minus_half"] = a.take(10)
    V["S"] = a.take(CC * HD)
    for name, w in (("idx", 2 * NT), ("top_w", 2 * NT)):
        V[name] = a.take(w)
    V["base_end"] = a.at

    V["bias"] = a.take(QH * KEYS)
    V["bias_v"] = split(V["bias"], QH)
    V["bias_first"] = split(a.take(QH * 64), QH)
    V["rksel"] = split(a.take(2 * CC), CC)
    V["w2"], V["g2"] = a.take(C), a.take(C)
    w_in_at = a.at
    V["w_in"] = split(a.take(KD * IN_COLS), KD)
    for name, w in (("raw", NF * (P + 1)), ("qkv0", 768), ("qkv1", 768), ("Pb", 8 * 65), ("kT", 2 * KEYS), ("Pm", 1024)):
        V[name] = a.take(w)
    V["raw_v"], V["kT_v"], V["Pm_v"] = split(V["raw"], NF), split(V["kT"], 2), split(V["Pm"], 4)
    V["Pb_v"] = split(V["Pb"], 8)
    V["qkv"] = [V["qkv0"], V["qkv1"]]
    tail = a.at
    for name, w in (("x", D), ("junk", D), ("hT", D), ("ssx", 1), ("msx", 1), ("rsx", 1), ("delta", C), ("f0", NF * P),
                    ("f1", NF * P), ("tw", P), ("sg", P), ("sw", C), ("sa", C), ("kk", C), ("sq", C), ("ssm", 8),
                    ("ninv", 8), ("nT", P), ("cum", C), ("Pinv", C), ("kp", C),
                    ("ms10", 10), ("rs10", 10), ("qn", C + 256), ("kn", P), ("qT", C), ("L", 4 * KEYS), ("negm", 8),
                    ("sd", 8), ("sm", 8), ("es", 8), ("den", 8), ("PT", 1024), ("pk_all", NPK)):
        V[name] = a.take(w)
    V["hT"] = split(V["hT"], KD)
    V["sqk"], V["bb"], V["rk"] = V["junk"][:, 0:640], V["sw"], V["sq"]
    V["f"] = [split(V["f0"], NF), split(V["f1"], NF)]
    V["delta"], V["L"], V["PT"] = split(V["delta"], 4), split(V["L"], 4), split(V["PT"], 4)
    V["pk"] = {n: V["pk_all"][:, lo:hi] for n, (lo, hi) in PK.items()}
    V["pk"]["AR_v"] = V["pk"]["AR"].rearrange("p (c e n) -> p c e n", c=CC, e=2)
    assert a.at <= total, a.at

    s = Arena(arena, tail)
    V["ada_slots"] = [split(s.take(KD * 512), KD) for _ in range(2)]
    for name, w in (("csig", KD), ("cs", KD), ("cs_rows", KD * P), ("gt", 2 * D)):
        V[name] = s.take(w)
    V["cs_rows"] = split(V["cs_rows"], KD)
    s = Arena(arena, w_in_at)
    V["onehot"], V["rel_bias"], V["gate_b"] = s.take(2 * CHUNK * CHUNK), s.take(QH), s.take(2 * D)
    return V, arena, total


_LV = range(1, len(LEVELS))
USES2 = {"Z0": ("M0", "M4", *(f"z{l}" for l in _LV), "G", "U0", "U1"),
         "Z1": ("M1", "M5", *(f"z{l}" for l in _LV), "I", "U0", "U1"),
         "X0": ("M2", "M6", "t0", *[f"{k}{l}" for l in _LV for k in "xt"][:-1], "WT"),
         "X1": ("M3", "M7", "t0", *[f"{k}{l}" for l in _LV for k in "xt"][:-1], "D0", "D1"),
         "YE": ("y",), "YO": ("y",),
         "O0": ("yT", "o", "hT", "rl"), "O1": ("yT", "o", "hT")}
BANK2 = {b: i for i, b in enumerate(("O0", "O1", "Z0", "Z1", "X0", "X1", "YE", "YO"))}


def views2(V, arena, total):
    a = Arena(arena, V["base_end"])
    for name, w in (("w_out", KD * D), ("w_router", KD * NR), ("gt1", D), ("pk0", NPK), ("pk1", NPK), ("MT", 4 * P * H),
                    ("X", P * H), ("XT", P * H), ("Z", P * H), ("ET0", P * H), ("ET1", P * H), ("G", C), ("U0", C),
                    ("WT", C), ("U", C), ("Stmp", C // 2), ("mu", 8), ("var", 8), ("rsy", 8), ("yc", C), ("sqy", C),
                    ("vb", C), ("yT", D), ("tmp", D), ("x1", D), ("xn2", D), ("h2T", D), ("junk2", D), ("ss2", 1),
                    ("ms2", 1), ("rs2", 1), ("g8", 8), ("m8", 8), ("i8", 8), ("gid", 1), ("ngm", 1), ("ge", 4), ("gs", 1),
                    ("ex", NE), ("eq", NE), ("off", NE), ("e8", 8), ("ei8", 8), ("dd", 1), ("de", 1), ("w0_", 1)):
        V["2" + name] = a.take(w)
    assert a.at <= total, a.at
    W = {n[1:]: v for n, v in V.items() if n[0] == "2"}
    for n in ("w_out", "w_router", "yT", "h2T"):
        W[n] = split(W[n], KD)
    for n in ("MT", "X", "XT", "Z", "ET0", "ET1"):
        W[n] = split(W[n], H)
    W["ET"] = [W["ET0"], W["ET1"]]
    W["pk"] = []
    for b in range(2):
        pk = {n: W[f"pk{b}"][:, lo:hi] for n, (lo, hi) in PK.items()}
        pk["AR"] = pk["AR"].rearrange("p (c e n) -> p c e n", c=CC, e=2)
        W["pk"].append(pk)
    for n in ("i8", "ei8"):
        W[n] = W[n].bitcast(U32)
    return W


def pass2(nc, S, ps, V, W, ins, dram, nt):
    B = Banks(S, "b", USES2, nt, ahead=sum((USES2[b] for b in ("Z0", "Z1", "X0", "X1", "YE")), ()))
    bank = {b: ps[i] for b, i in BANK2.items()}
    k, row = V["k"], V["row"]
    ident, level = k("ident"), split(k("level"), len(LEVELS))
    MT, X, XT, Z, ET = W["MT"], W["X"], W["XT"], W["Z"], W["ET"]
    St = split(V["S"], CC)
    half = lambda h: (64 * (h % 2), h // 2)
    hs = lambda h: slice(HD * h, HD * h + HD)
    by_head = lambda ap: ap.rearrange("p (c e n) -> p c e n", c=CC, e=2)
    M_BANKS = ("Z0", "Z1", "X0", "X1")
    last = len(LEVELS) - 1

    ORDER = (("M", 1), ("nrm", 0), ("x2", 1), ("lvl1", 1), ("yT", 0), ("load", 2), ("lvl2", 1), ("o0", 0), ("lvl3", 1),
             ("o1", 0), ("res", 0), ("lvl4", 1), ("norm2", 0), ("lvl5", 1), ("h2T", 0), ("W", 1), ("route", 0),
             ("S0", 1), ("S1", 1))

    def run(eng, steps):
        def tile(t, parity, front=True, back=True):
            for name, ahead in ORDER:
                if (front if ahead else back) and name in steps:
                    steps[name](t + ahead, (parity + ahead) % 2)

        tile(-1, 1, back=False)
        tile(0, 0)
        tile(1, 1)
        if nt > 4:
            with eng.Fori(1, nt // 2 - 1) as u:
                tile(2 * u, 0)
                tile(2 * u + 1, 1)
        tile(nt - 2, 0)
        tile(nt - 1, 1, front=False)

    with nc.Block() as block:
        @block.sync
        def _(sp):
            def load(n, b):
                if isinstance(n, int) and n >= nt:
                    return
                B.wait_full(sp, "O1", "yT", n - 2)
                sp.dma_start(W[f"pk{b}"], dram["mid"][bass.ds(n, 1)].rearrange("a p n -> (a p) n")).then_inc(S[f"pack{b}"], 16)

            def residual(t, b):
                S.wait(sp, "x1_out", 16 * t)
                S.wait(sp, "xn2", t)
                sp.dma_start(W["x1"], dram["x"][bass.ds(t * P, P), :]).then_inc(S["xres"], 16)

            def store_x1(t, b):
                S.wait(sp, "x1", t + 1)
                sp.dma_start(dram["x1"][bass.ds(t * P, P), :], W["x1"]).then_inc(S["x1_out"], 16)

            def store_xn2(t, b):
                S.wait(sp, "xn2", t + 1)
                sp.dma_start(dram["xn2"][bass.ds(t * P, P), :], W["xn2"]).then_inc(S["xn2_out"], 16)

            load(0, 0)
            sp.dma_start(W["w_out"], ins["w_out"].rearrange("(k p) n -> p k n", p=P)).then_inc(S["w_out"], 16)
            sp.dma_start(W["w_router"], ins["w_router"].rearrange("(k p) n -> p k n", p=P)).then_inc(S["w_out"], 16)
            sp.dma_start(W["gt1"], dram["gates"][:, 0:D]).then_inc(S["w_out"], 16)
            run(sp, {"load": load, "nrm": residual, "res": store_x1, "norm2": store_xn2})
            sp.wait_ge(S["zero_row"], 1)
            sp.dma_start(dram["xn2"][T:T + 1, :], W["junk2"][0:1, :]).then_inc(S["xn2_out"], 16)
            sp.wait_ge(S["xn2_out"], 16 * nt + 16)
            sp.wait_ge(S["x1_out"], 16 * nt)

        @block.tensor
        def _(pe):
            def wait_pack(n, b):
                S.wait(pe, f"pack{b}", 16 * (n // 2) + 16 if isinstance(n, int) else 8 * (n - b) + 16)

            def M(n, b):
                wait_pack(n, b)
                pk = W["pk"][b]
                for h in range(H):
                    hp, c = half(h)
                    name = M_BANKS[h % 4]
                    B.wait_free(pe, name, f"M{h}", n)
                    ar = pk["AR"][hp:hp + 64, c, :, :].rearrange("p e n -> p (e n)")
                    for i, f in enumerate(("BT", "KT")):
                        mm = pe.matmul(bank[name][:, 256 * i:256 * i + 256], pk[f][hp:hp + 64, P * c:P * c + P], ar,
                                       start=True, stop=True)
                    B.full(mm, name)

            def turn(n, use, wait):
                for g in range(2):
                    wait(g)
                    B.wait_free(pe, f"X{g}", use, n)
                    for i in range(4):
                        src = XT if use == "t0" else X
                        mm = pe.transpose(bank[f"X{g}"][:, P * i:P * i + P], src[:, 4 * g + i, :], ident)
                    B.full(mm, f"X{g}")

            def x2(n, b):
                turn(n, "t0", lambda g: S.wait(pe, "xt2", n + 1))

            def lvl(l):
                def go(n, b):
                    S.wait(pe, "et", 6 * n + l + 1)
                    for g in range(2):
                        B.wait_read(pe, f"X{g}", f"t{l - 1}", n)
                        B.wait_free(pe, f"Z{g}", f"z{l}", n)
                        for i in range(4):
                            h = 4 * g + i
                            mm = pe.matmul(bank[f"Z{g}"][:, P * i:P * i + P], ET[l % 2][:, h, :], X[:, h, :],
                                           start=True, stop=True)
                        B.full(mm, f"Z{g}")
                    for g in range(2):
                        B.wait_read(pe, f"Z{g}", f"z{l}", n)
                        B.wait_free(pe, f"X{g}", f"x{l}", n)
                        for i in range(4):
                            h = 4 * g + i
                            a, c = (Z, XT) if l == last else (XT, Z)
                            mm = pe.matmul(bank[f"X{g}"][:, P * i:P * i + P], a[:, h, :], c[:, h, :],
                                           start=True, stop=True)
                        B.full(mm, f"X{g}")
                    if l < last:
                        turn(n, f"t{l}", lambda g: B.wait_read(pe, f"X{g}", f"x{l}", n))
                return go

            def Wstep(n, b):
                pk = W["pk"][b]
                B.wait_free(pe, "Z0", "G", n)
                for h in range(H):
                    mm = pe.matmul(bank["Z0"][:, hs(h)], MT[:, h, 256:384], pk["V"][:, hs(h)], start=True, stop=True)
                B.full(mm, "Z0")
                for g in range(2):
                    B.wait_read(pe, f"X{g}", f"x{last}", n)
                B.wait_free(pe, "X0", "WT", n)
                for h in range(H):
                    hp, c = half(h)
                    mm = pe.matmul(bank["X0"][hp:hp + 64, P * c:P * c + P], pk["A"][:, hs(h)], XT[:, h, :],
                                   start=True, stop=True)
                B.full(mm, "X0")
                B.wait_read(pe, "Z0", "G", n)
                B.wait_free(pe, "Z1", "I", n)
                for h in range(H):
                    mm = pe.matmul(bank["Z1"][:, hs(h)], XT[:, h, :], W["G"][:, hs(h)], start=True, stop=True)
                B.full(mm, "Z1")

            def scan(q):
                rows = slice(64 * q, 64 * q + 64)

                def go(n, b):
                    pk = W["pk"][b]
                    if q == 0:
                        for e, name in enumerate(("YE", "YO")):
                            B.wait_free(pe, name, "y", n)
                            for c in range(CC):
                                h = 2 * c + e
                                pe.matmul(bank[name][:, hs(c)], MT[:, h, 384:512], pk["V"][:, hs(h)],
                                          start=(c == 0), stop=False, skip_group_check=True)
                        B.wait_read(pe, "X0", "WT", n)
                    S.wait(pe, "state", 2 * n + q)
                    for e, name in enumerate(("Z0", "Z1")):
                        B.wait_free(pe, name, f"U{q}", n)
                        pe.sem_inc(S["pe_passed"], 1)
                        for c in range(CC):
                            hp = 64 * e
                            mm = pe.matmul(bank[name][rows, hs(c)], W["WT"][hp:hp + 64, P * c + 64 * q:P * c + 64 * q + 64],
                                           St[hp:hp + 64, c, :], start=True, stop=True)
                        B.full(mm, name)
                    for e, name in enumerate(("YE", "YO")):
                        for c in range(CC):
                            hp = 64 * e
                            pe.matmul(bank[name][rows, hs(c)], pk["AR"][hp:hp + 64, c, 1, rows],
                                      St[hp:hp + 64, c, :], start=False, stop=False, skip_group_check=True)
                    B.wait_free(pe, "X1", f"D{q}", n)
                    for e in range(2):
                        B.wait_read(pe, f"Z{e}", f"U{q}", n)
                    pe.sem_inc(S["pe_passed"], 1)
                    for h in range(H):
                        hp, c = half(h)
                        for i, (f, rhs) in enumerate((("B", W["U"]), ("K", pk["V"]))):
                            mm = pe.matmul(bank["X1"][hp:hp + 64, hs(c)], pk[f][rows, hs(h)], rhs[rows, hs(h)],
                                           start=(i == 0), stop=(i == 1))
                    B.full(mm, "X1")
                    if q == 1:
                        for e, name in enumerate(("YE", "YO")):
                            for c in range(CC):
                                h = 2 * c + e
                                mm = pe.matmul(bank[name][:, hs(c)], MT[:, h, 128:256], W["U"][:, hs(h)],
                                               start=False, stop=(c == CC - 1), skip_group_check=True)
                            B.full(mm, name)
                return go

            def yT(t, b):
                pk = W["pk"][b]
                for name, src in (("O1", pk["ya"]), ("O0", W["yc"])):
                    B.wait_free(pe, name, "yT", t)
                    if name == "O0":
                        S.wait(pe, "yr", t + 1)
                    for c in range(CC):
                        mm = pe.transpose(bank[name][:, P * c:P * c + P], src[:, P * c:P * c + P], ident)
                    B.full(mm, name)

            def o(n0):
                def go(t, b):
                    name = f"O{n0}"
                    for other in ("O0", "O1"):
                        B.wait_read(pe, other, "yT", t)
                    for kk in range(KD):
                        mm = pe.matmul(bank[name][:, :], W["yT"][:, kk, :], W["w_out"][:, kk, 512 * n0:512 * n0 + 512],
                                       start=(kk == 0), stop=(kk == KD - 1))
                    B.full(mm, name)
                return go

            def h2T(t, b):
                S.wait(pe, "xn2", t + 1)
                for g in range(2):
                    B.wait_free(pe, f"O{g}", "hT", t)
                    for i in range(4):
                        c = 4 * g + i
                        mm = pe.transpose(bank[f"O{g}"][:, P * i:P * i + P], W["xn2"][:, P * c:P * c + P], ident)
                    B.full(mm, f"O{g}")

            def route(t, b):
                B.wait_read(pe, "O1", "hT", t)
                B.wait_free(pe, "O0", "rl", t)
                for kk in range(KD):
                    mm = pe.matmul(bank["O0"][:, 0:NR], W["h2T"][:, kk, :], W["w_router"][:, kk, :],
                                   start=(kk == 0), stop=(kk == KD - 1))
                B.full(mm, "O0")

            pe.wait_ge(S["w_out"], 48)
            run(pe, {"M": M, "x2": x2, **{f"lvl{l}": lvl(l) for l in _LV}, "W": Wstep, "S0": scan(0), "S1": scan(1),
                     "yT": yT, "o0": o(0), "o1": o(1), "h2T": h2T, "route": route})

        @block.scalar
        def _(act):
            def turned(n, use, dst):
                for g in range(2):
                    B.wait_full(act, f"X{g}", use, n)
                    B.free(act.activation(dst[:, 4 * g:4 * g + 4, :], split(bank[f"X{g}"][:, :], 4), ACT.Copy), f"X{g}")

            def x2(n, b):
                turned(n, "t0", X)

            def lvl(l):
                def go(n, b):
                    for g in range(2):
                        B.wait_full(act, f"Z{g}", f"z{l}", n)
                        B.free(act.activation(Z[:, 4 * g:4 * g + 4, :], split(bank[f"Z{g}"][:, :], 4), ACT.Copy), f"Z{g}")
                    if l < last:
                        turned(n, f"t{l}", XT)
                return go

            def Wstep(n, b):
                for name, use, dst in (("Z0", "G", "G"), ("X0", "WT", "WT")):
                    B.wait_full(act, name, use, n)
                    B.free(act.activation(W[dst], bank[name][:, :], ACT.Copy), name)

            def nrm(t, b):
                S.wait(act, "yc", t + 1)
                act.activation(W["sqy"], W["yc"], ACT.Square).then_inc(S["sqy"], 1)

            def yT(t, b):
                for i, name in ((1, "O1"), (0, "O0")):
                    B.wait_full(act, name, "yT", t)
                    B.free(act.activation(W["yT"][:, 4 * i:4 * i + 4, :], split(bank[name][:, :], 4), ACT.Copy), name)

            def norm2(t, b):
                S.wait(act, "x1", t + 1)
                act.activation(W["junk2"], W["x1"], ACT.Square, accum_out=W["ss2"]).then_inc(S["ss2"], 1)

            def h2T(t, b):
                for g in range(2):
                    B.wait_full(act, f"O{g}", "hT", t)
                    for i in range(4):
                        c = 4 * g + i
                        a = act.activation(W["h2T"][:, c, :], bank[f"O{g}"][:, P * i:P * i + P], ACT.Identity,
                                           scale=V["s2"][:, c:c + 1], bias=V["b2"][:, c:c + 1])
                    B.free(a, f"O{g}")

            def route(t, b):
                S.wait(act, "ngm", t + 1)
                act.activation(W["ge"], W["g8"][:, 0:NG], ACT.Exp, bias=W["ngm"][:, 0:1], accum_out=W["gs"])
                S.wait(act, "dd", t + 1)
                act.activation(W["de"], W["dd"], ACT.Exp).then_inc(S["de"], 1)

            run(act, {"x2": x2, **{f"lvl{l}": lvl(l) for l in _LV}, "W": Wstep, "nrm": nrm, "yT": yT, "norm2": norm2,
                      "h2T": h2T, "route": route})
            act.drain()
            act.activation(W["junk2"][0:1, :], W["x1"][0:1, :], ACT.Copy, scale=0.0).then_inc(S["zero_row"], 1)

        @block.gpsimd
        def _(pool):
            def et(l):
                def go(n, b):
                    if l == 0:
                        B.wait_read(pool, "X1", "M7", n)
                    if l >= 2:
                        B.wait_full(pool, "Z1", f"z{l - 2}", n) if l > 2 else S.wait(pool, "xt2", n + 1)
                    pool.tensor_tensor(ET[l % 2], MT[:, :, 0:P], level[:, l:l + 1, :].to_broadcast([P, H, P]),
                                       ALU.mult).then_inc(S["et"], 1)
                return go

            def x2(n, b):
                for l in range(2):
                    et(l)(n, b)

            def nrm(t, b):
                S.wait(pool, "vary", t + 1)
                pool.tensor_tensor(W["rsy"], W["var"], V["minus_half"][:, 0:8], ALU.pow).then_inc(S["rsy"], 1)
                B.wait_full(pool, "O1", "yT", t - 1)
                pool.tensor_tensor(split(W["vb"], H), split(W["pk"][b]["V"], H), per_channel(W["pk"][b]["bon"], HD),
                                   ALU.mult).then_inc(S["vb"], 1)

            def norm2(t, b):
                S.wait(pool, "ms2", t + 1)
                pool.tensor_tensor(W["rs2"], W["ms2"], V["minus_half"][:, 0:1], ALU.pow).then_inc(S["rs2"], 1)

            pool.memset(W["g8"], NEG).then_inc(S["g8_fill"], 1)
            run(pool, {"x2": x2, **{f"lvl{l - 1}": et(l) for l in _LV if l >= 2}, "nrm": nrm, "norm2": norm2})

        @block.vector
        def _(dve):
            def M(n, b):
                for h in range(H):
                    name = M_BANKS[h % 4]
                    B.wait_full(dve, name, f"M{h}", n)
                    B.free(dve.tensor_tensor(MT[:, h, :], bank[name][:, :], k("mmask"), ALU.mult), name)

            def x2(n, b):
                S.wait(dve, "et", 6 * n + 1)
                dve.tensor_tensor(XT, ET[0], ident.unsqueeze(1).to_broadcast([P, H, P]), ALU.add).then_inc(S["xt2"], 1)

            def lvl(l):
                dst = XT if l == last else X

                def go(n, b):
                    for g in range(2):
                        B.wait_full(dve, f"X{g}", f"x{l}", n)
                        d = dst[:, 4 * g:4 * g + 4, :]
                        B.free(dve.tensor_tensor(d, d, split(bank[f"X{g}"][:, :], 4), ALU.add), f"X{g}")
                return go

            def Wstep(n, b):
                B.wait_full(dve, "Z1", "I", n)
                B.free(dve.tensor_copy(W["U0"], bank["Z1"][:, :]), "Z1")

            def scan(q):
                rows = slice(64 * q, 64 * q + 64)

                def go(n, b):
                    if q == 0:
                        dve.drain()
                    for e in range(2):
                        B.wait_full(dve, f"Z{e}", f"U{q}", n)
                        B.free(dve.tensor_tensor(by_head(W["U"])[rows, :, e, :], split(bank[f"Z{e}"][rows, 0:256], CC),
                                                 by_head(W["U0"])[rows, :, e, :], ALU.add), f"Z{e}")
                    B.wait_full(dve, "X1", f"D{q}", n)
                    B.free(dve.tensor_tensor(W["Stmp"], V["S"], bank["X1"][:, 0:256], ALU.add), "X1")
                    dve.drain()
                    pc = W["pk"][b]["PC"].rearrange("p (c q) -> p c q", q=2)[:, :, q:q + 1].to_broadcast([P, CC, HD])
                    dve.tensor_tensor(St, split(W["Stmp"], CC), pc, ALU.mult).then_inc(S["state"], 1)
                return go

            def nrm(t, b):
                pk = W["pk"][b]
                mu = W["mu"].rearrange("p (c e) -> p c e", e=2)
                yc = by_head(W["yc"])
                for e, name in enumerate(("YE", "YO")):
                    B.wait_full(dve, name, "y", t)
                    dve.tensor_reduce(mu[:, :, e:e + 1], split(bank[name][:, 0:256], CC), AX.X, ALU.add)
                dve.drain()
                dve.tensor_scalar(W["mu"], W["mu"], 1.0 / HD, None, ALU.mult)
                dve.drain()
                B.wait_full(dve, "O0", "yT", t - 1)
                for e, name in enumerate(("YE", "YO")):
                    B.free(dve.tensor_tensor(yc[:, :, e, :], split(bank[name][:, 0:256], CC),
                                             mu[:, :, e:e + 1].to_broadcast([P, CC, HD]), ALU.subtract), name)
                dve.engine_nop().then_inc(S["yc"], 1)
                S.wait(dve, "sqy", t + 1)
                dve.tensor_reduce(W["var"], split(W["sqy"], H), AX.X, ALU.add)
                dve.drain()
                dve.tensor_scalar(W["var"], W["var"], 1.0 / HD, 64e-5, ALU.mult, ALU.add).then_inc(S["vary"], 1)
                S.wait(dve, "rsy", t + 1)
                dve.tensor_tensor(split(W["yc"], H), split(W["yc"], H), per_channel(W["rsy"], HD), ALU.mult)
                dve.drain()
                dve.tensor_tensor(W["yc"], W["yc"], row("ln_w"), ALU.mult)
                dve.drain()
                dve.tensor_tensor(W["yc"], W["yc"], row("ln_b"), ALU.add)
                dve.drain()
                S.wait(dve, "vb", t + 1)
                dve.tensor_tensor(W["yc"], W["yc"], W["vb"], ALU.add)
                dve.drain()
                dve.tensor_tensor(W["yc"], W["yc"], pk["gate"], ALU.mult).then_inc(S["yr"], 1)

            def res(t, b):
                S.wait(dve, "xres", 16 * t + 16)
                for n0 in range(2):
                    cols = slice(512 * n0, 512 * n0 + 512)
                    B.wait_full(dve, f"O{n0}", "o", t)
                    B.free(dve.tensor_tensor(W["tmp"][:, cols], bank[f"O{n0}"][:, :], W["gt1"][:, cols], ALU.mult), f"O{n0}")
                dve.drain()
                dve.tensor_tensor(W["x1"], W["x1"], W["tmp"], ALU.add).then_inc(S["x1"], 1)

            def norm2(t, b):
                S.wait(dve, "ss2", t + 1)
                dve.tensor_scalar(W["ms2"], W["ss2"], 1.0 / D, 1e-6, ALU.mult, ALU.add).then_inc(S["ms2"], 1)
                S.wait(dve, "rs2", t + 1)
                S.wait(dve, "xn2_out", 16 * t)
                B.wait_full(dve, "O1", "hT", t - 1)
                dve.tensor_scalar(W["xn2"], W["x1"], W["rs2"][:, 0:1], None, ALU.mult).then_inc(S["xn2"], 1)

            def route(t, b):
                rb = row("rb")
                S.wait(dve, "de", t)
                B.wait_full(dve, "O0", "rl", t)
                dve.tensor_tensor(W["g8"][:, 0:NG], bank["O0"][:, 0:NG], rb[:, 0:NG], ALU.add)
                B.free(dve.tensor_tensor(W["ex"], bank["O0"][:, NG:NR], rb[:, NG:NR], ALU.add), "O0")
                dve.drain()
                dve.max(W["m8"], W["g8"])
                dve.drain()
                dve.tensor_scalar(W["ngm"], W["m8"][:, 0:1], -1.0, None, ALU.mult).then_inc(S["ngm"], 1)
                dve.max_index(W["i8"], W["m8"], W["g8"])
                dve.drain()
                dve.tensor_copy(W["gid"], W["i8"][:, 0:1])
                dve.drain()
                dve.tensor_scalar(W["eq"], k("group_e"), W["gid"][:, 0:1], None, ALU.is_equal)
                dve.drain()
                dve.tensor_scalar(W["off"], W["eq"], 1.0, 1e30, ALU.subtract, ALU.mult)
                dve.tensor_tensor(W["ex"], W["ex"], W["eq"], ALU.mult)
                dve.drain()
                dve.tensor_tensor(W["ex"], W["ex"], W["off"], ALU.add)
                dve.drain()
                dve.max(W["e8"], W["ex"])
                dve.drain()
                dve.tensor_tensor(W["dd"], W["e8"][:, 1:2], W["e8"][:, 0:1], ALU.subtract).then_inc(S["dd"], 1)
                dve.max_index(W["ei8"], W["e8"], W["ex"])
                dve.drain()
                dve.tensor_copy(V["idx"][:, bass.ds(2 * t, 2)], W["ei8"][:, 0:2])
                S.wait(dve, "de", t + 1)
                dve.scalar_tensor_tensor(W["w0_"], W["de"], 1.0, W["gs"], ALU.add, ALU.mult)
                dve.drain()
                dve.reciprocal(W["w0_"], W["w0_"])
                dve.drain()
                dve.tensor_copy(V["top_w"][:, bass.ds(2 * t, 1)], W["w0_"])
                dve.tensor_tensor(V["top_w"][:, bass.ds(2 * t + 1, 1)], W["w0_"], W["de"], ALU.mult)

            dve.wait_ge(S["g8_fill"], 1)
            dve.wait_ge(S["w_out"], 48)
            run(dve, {"M": M, "x2": x2, **{f"lvl{l}": lvl(l) for l in _LV}, "W": Wstep, "S0": scan(0), "S1": scan(1),
                      "nrm": nrm, "res": res, "norm2": norm2, "route": route})


SLOTS = 3
SLOT = 3 * KD * FE


def views3(V, arena, total):
    a = Arena(arena, V["base_end"])
    W = {}
    for name, w in (("slots", SLOTS * SLOT), ("gt2", D), ("xT", D), ("h", FE), ("hT", FE), ("xg", D), ("ysb", D),
                    ("sg", FE), ("dest", 2 * NT), ("row_tok", NB + 1), ("idx_now", 1), ("tab", 2 * NB + NE), ("nblk", 1)):
        W[name] = a.take(w)
    W["idx_now2"] = [a.take(2).bitcast(U32) for _ in range(2)]
    for name in ("dest", "idx_now"):
        W[name] = W[name].bitcast(U32)
    for name in ("row_tok", "tab", "nblk"):
        W[name] = W[name].bitcast(I32)
    at = a.at
    for name, w in (("oh0", NT * NE), ("oh1", NT * NE), ("ohs", NT * NE), ("pre", (NT + 1) * NE)):
        W[name] = a.take(w)
    for name in ("cnt", "nb", "nbi", "eb", "pend", "pstart"):
        W[name] = a.take(NE)
    for name in ("destf", "desti", "lo", "hi", "lof", "hif", "pos", "tokI"):
        W[name] = a.take(2 * NT)
    for name in ("be", "bei", "bef", "m3", "m3f"):
        W[name] = a.take(NB)
    assert a.at <= total, (a.at, at)
    W["cmp"] = arena[:, V["base_end"] + SLOTS * SLOT + D:V["base_end"] + SLOTS * SLOT + D + NB * NE]
    for name in ("nbi", "desti", "lo", "hi", "tokI", "bei", "m3"):
        W[name] = W[name].bitcast(I32)
    W["pos"] = W["pos"].bitcast(U32)
    return W


def dispatch(nc, S, ps, V, W, ins, dram):
    k = V["k"]
    te = lambda ap: ap.rearrange("p (t e) -> p t e", e=NE)
    idx = V["idx"].rearrange("p (t c) -> p t c", c=2)
    with nc.Block() as block:
        @block.sync
        def _(sp):
            for e in range(SLOTS):
                load_expert(sp, S, W, ins, e, e)
            sp.dma_start(W["gt2"], dram["gates"][:, D:2 * D]).then_inc(S["gt2"], 16)
            sp.wait_ge(S["fill"], 1)
            sp.dma_start(dram["row_tok"].rearrange("(p b) o -> p (b o)", p=P), W["row_tok"]).then_inc(S["filled"], 16)
            sp.wait_ge(S["tok_rows"], 16 * 2 * NT)
            sp.dma_start(W["row_tok"], dram["row_tok"].rearrange("(p b) o -> p (b o)", p=P)).then_inc(S["filled"], 16)
            sp.wait_ge(S["filled"], 32)

        @block.gpsimd
        def _(pool):
            pool.memset(W["row_tok"], T).then_inc(S["fill"], 1)
            pool.wait_ge(S["filled"], 16)
            pool.wait_ge(S["pos"], 1)
            for i in range(2 * NT):
                pool.indirect_dma_start(dram["row_tok"], bass.IndirectOffsetOnAxis(ap=W["pos"][:, i:i + 1], axis=0),
                                        W["tokI"][:, i:i + 1], None).then_inc(S["tok_rows"], 16)
            pool.wait_ge(S["tok_rows"], 16 * 2 * NT)

        @block.tensor
        def _(pe):
            pe.wait_ge(S["pre"], 1)
            pe.matmul(ps[0][:, :], k("before"), W["ohs"], start=True, stop=False)
            pe.matmul(ps[0][:, :], k("ones"), W["pre"][:, 0:NT * NE], start=False, stop=True)
            pe.matmul(ps[1][:, 0:NE], k("ones"), W["pre"][:, NT * NE:], start=True, stop=True).then_inc(S["rank"], 1)

        @block.vector
        def _(dve):
            def do(ins, wait=True):
                if wait:
                    dve.drain()

            iota = k("iota_e").unsqueeze(1).to_broadcast([P, NT, NE])
            for c in range(2):
                dve.tensor_tensor(te(W[f"oh{c}"]), iota, idx[:, :, c:c + 1].to_broadcast([P, NT, NE]), ALU.is_equal)
            dve.memset(W["pre"][:, 0:NE], 0.0)
            do(dve.tensor_copy(W["tokI"].rearrange("p (t c) -> p t c", c=2), per_channel(k("token"), 2)))
            do(dve.tensor_tensor(W["ohs"], W["oh0"], W["oh1"], ALU.add))
            for t in range(NT):
                a = slice(NE * t, NE * t + NE)
                i = dve.tensor_tensor(W["pre"][:, NE * t + NE:NE * t + 2 * NE], W["pre"][:, a], W["ohs"][:, a], ALU.add)
                if t == NT - 1:
                    i.then_inc(S["pre"], 1)
                else:
                    dve.drain()
            dve.wait_ge(S["rank"], 1)
            do(dve.tensor_scalar(W["cnt"], ps[1][:, 0:NE], float(P - 1), None, ALU.add))
            do(dve.tensor_copy(W["nbi"], W["cnt"]))
            do(dve.tensor_scalar(W["nbi"], W["nbi"], 7, None, ALU.arith_shift_right))
            do(dve.tensor_copy(W["nb"], W["nbi"]))
            do(dve.tensor_tensor_scan(W["eb"], k("ones")[:, 0:NE], W["nb"], 0.0, ALU.mult, ALU.add))
            dve.tensor_scalar(W["pend"], W["eb"], float(P), None, ALU.mult)
            do(dve.tensor_tensor(W["pstart"], W["eb"], W["nb"], ALU.subtract))
            do(dve.tensor_scalar(W["pstart"], W["pstart"], float(P), None, ALU.mult))
            do(dve.tensor_tensor(te(W["ohs"]), te(ps[0][:, :]), W["pstart"].unsqueeze(1).to_broadcast([P, NT, NE]), ALU.add))
            for c in range(2):
                dve.tensor_tensor(W[f"oh{c}"], W[f"oh{c}"], W["ohs"], ALU.mult)
            dve.drain()
            destf = W["destf"].rearrange("p (t c) -> p t c", c=2)
            for c in range(2):
                dve.tensor_reduce(destf[:, :, c:c + 1], te(W[f"oh{c}"]), AX.X, ALU.add)
            dve.drain()
            dve.tensor_copy(W["dest"], W["destf"])
            do(dve.tensor_copy(W["desti"], W["destf"]))
            dve.tensor_scalar(W["lo"], W["desti"], P - 1, None, ALU.bitwise_and)
            do(dve.tensor_scalar(W["hi"], W["desti"], 7, None, ALU.arith_shift_right))
            dve.tensor_copy(W["lof"], W["lo"])
            do(dve.tensor_copy(W["hif"], W["hi"]))
            do(dve.scalar_tensor_tensor(W["destf"], W["lof"], float(NB + 1), W["hif"], ALU.mult, ALU.add))
            dve.tensor_copy(W["pos"], W["destf"]).then_inc(S["pos"], 1)
            be3 = W["cmp"].rearrange("p (b e) -> p b e", e=NE)
            do(dve.tensor_tensor(be3, W["pend"].unsqueeze(1).to_broadcast([P, NB, NE]), per_channel(k("block_row"), NE),
                                 ALU.is_le))
            do(dve.tensor_reduce(W["be"], be3, AX.X, ALU.add))
            do(dve.tensor_scalar(W["be"], W["be"], float(NE - 1), None, ALU.min))
            do(dve.tensor_scalar(W["bef"], W["be"], 11.0, None, ALU.mult))
            do(dve.tensor_copy(W["bei"], W["bef"]))
            do(dve.tensor_scalar(W["m3"], W["bei"], 5, None, ALU.arith_shift_right))
            do(dve.tensor_copy(W["m3f"], W["m3"]))
            do(dve.scalar_tensor_tensor(W["m3f"], W["m3f"], -float(SLOTS), W["be"], ALU.mult, ALU.add))
            dve.tensor_scalar(W["tab"][:, 0:NB], W["m3f"], float(SLOT), None, ALU.mult)
            dve.tensor_scalar(W["tab"][:, NB:2 * NB], W["be"], 48.0, 48.0, ALU.mult, ALU.add)
            dve.tensor_scalar(W["tab"][:, 2 * NB:], W["eb"], 1.0, None, ALU.add)
            dve.tensor_copy(W["nblk"], W["eb"][:, NE - 1:NE])


def load_expert(eng, S, W, ins, e, slot):
    S.wait(eng, "weights", 48 * e)
    if not isinstance(e, int):
        eng.sem_inc(S["sp_passed"], 1)
    base = W["slots"][:, SLOT * slot:SLOT * slot + SLOT]
    for i, (name, rows) in enumerate((("w1", KD), ("w3", KD), ("w2e", FE // P))):
        src = ins[name][bass.ds(e, 1)].rearrange("a (k p) n -> p (a k) n", p=P)
        eng.dma_start(split(base[:, KD * FE * i:KD * FE * i + KD * FE], rows), src).then_inc(S["weights"], 16)


def experts(nc, S, ps, V, W, ins, dram):
    ident = V["k"]("ident")
    bank = dict(zip(("HA", "HB", "HT", "X0", "X1", "Y0", "Y1"), ps))
    xT, hT, h = split(W["xT"], KD), split(W["hT"], FE // P), W["h"]
    with nc.Block() as block:
        @block.sync
        def _(sp):
            def load(e, slot):
                done = sp.value_load(W["tab"][0:1, bass.ds(2 * NB + e - SLOTS, 1)], min_val=1, max_val=NB + 1)
                sp.wait_ge(S["blocks_done"], done)
                sp.sem_inc(S["sp_passed"], 1)
                load_expert(sp, S, W, ins, e, slot)

            with sp.Fori(1, NE // SLOTS) as j:
                for i in range(SLOTS):
                    load(SLOTS * j + i, i)
            for e in range(NE // SLOTS * SLOTS, NE):
                load(e, e % SLOTS)

        @block.gpsimd
        def _(pool):
            def gather(b):
                pool.tensor_copy(W["idx_now"].bitcast(I32), W["row_tok"][:, bass.ds(b, 1)])
                pool.drain()
                pool.indirect_dma_start(W["xg"], None, dram["xn2"],
                                        bass.IndirectOffsetOnAxis(ap=W["idx_now"], axis=0)).then_inc(S["xg"], 16)

            nblk = pool.value_load(W["nblk"][0:1, 0:1], min_val=1, max_val=NB)
            gather(0)
            with pool.Fori(0, NB) as b:
                with pool.If(b < nblk):
                    pool.wait_ge(S["x_turned"], b + 1)
                    gather(b + 1)

        @block.tensor
        def _(pe):
            def turn_x(b):
                pe.wait_ge(S["xg"], 16 * b + 16)
                for g in range(2):
                    for i in range(4):
                        c = 4 * g + i
                        mm = pe.transpose(bank[f"X{g}"][:, P * i:P * i + P], W["xg"][:, P * c:P * c + P], ident)
                mm.then_inc(S["x_turned"], 1)

            nblk = pe.value_load(W["nblk"][0:1, 0:1], min_val=1, max_val=NB)
            pe.sem_inc(S["blocks_done"], 1)
            turn_x(0)
            with pe.Fori(0, NB) as b:
                with pe.If(b < nblk):
                    slot = pe.value_load(W["tab"][0:1, bass.ds(b, 1)], min_val=0, max_val=(SLOTS - 1) * SLOT)
                    in_at = pe.value_load(W["tab"][0:1, bass.ds(b + NB, 1)], min_val=48, max_val=48 * NE)
                    w = lambda i, kk, n0, n: W["slots"][:, bass.ds(slot + KD * FE * i + kk + n0, n)]
                    pe.wait_ge(S["weights"], in_at)
                    pe.wait_ge(S["xT"], b + 1)
                    for g, name in enumerate(("HA", "HB")):
                        for i in range(2):
                            for kk in range(KD):
                                mm = pe.matmul(bank[name][:, 256 * i:256 * i + 256], xT[:, kk, :],
                                               w(i, FE * kk, 256 * g, 256), start=(kk == 0), stop=(kk == KD - 1))
                        mm.then_inc(S["up"], 1)
                    for g in range(2):
                        pe.wait_ge(S["h"], 2 * b + g + 1)
                        for i in range(2):
                            c = 2 * g + i
                            mm = pe.transpose(bank["HT"][:, P * c:P * c + P], h[:, P * c:P * c + P], ident)
                        mm.then_inc(S["h_turned"], 1)
                        pe.wait_ge(S["hT"], 2 * b + g + 1)
                        if g == 0:
                            pe.wait_ge(S["y_read"], b + 1)
                        for n0 in range(2):
                            for c in (2 * g, 2 * g + 1):
                                mm = pe.matmul(bank[f"Y{n0}"][:, :], hT[:, c, :], w(2, D * c, 512 * n0, 512),
                                               start=(c == 0), stop=(c == 3))
                        if g == 0:
                            turn_x(b + 1)
                    mm.then_inc(S["blocks_done"], 1)

        @block.scalar
        def _(act):
            def turned_x(b):
                act.wait_ge(S["x_turned"], b + 1)
                for c in range(KD):
                    a = act.activation(xT[:, c, :], bank[f"X{c // 4}"][:, P * (c % 4):P * (c % 4) + P], ACT.Identity,
                                       scale=V["s2"][:, c:c + 1], bias=V["b2"][:, c:c + 1])
                a.then_inc(S["xT"], 1)

            nblk = act.value_load(W["nblk"][0:1, 0:1], min_val=1, max_val=NB)
            act.sem_inc(S["y_out"], 16)
            turned_x(0)
            with act.Fori(0, NB) as b:
                with act.If(b < nblk):
                    for g, name in enumerate(("HA", "HB")):
                        act.wait_ge(S["up"], 2 * b + g + 1)
                        act.activation(W["sg"][:, 256 * g:256 * g + 256], bank[name][:, 0:256],
                                       ACT.Sigmoid).then_inc(S["sg"], 1)
                        if g == 1:
                            turned_x(b + 1)
                        act.wait_ge(S["h_turned"], 2 * b + g + 1)
                        act.activation(hT[:, 2 * g:2 * g + 2, :], split(bank["HT"][:, 256 * g:256 * g + 256], 2),
                                       ACT.Copy).then_inc(S["hT"], 1)
                    act.wait_ge(S["y_read"], b + 2)
                    act.sem_inc(S["act_passed"], 1)
                act.dma_start(dram["y"][bass.ds(b * P, P), :], W["ysb"]).then_inc(S["y_out"], 16)
            act.wait_ge(S["y_out"], 16 * NB + 16)

        @block.vector
        def _(dve):
            nblk = dve.value_load(W["nblk"][0:1, 0:1], min_val=1, max_val=NB)
            dve.sem_inc(S["y_read"], 1)
            with dve.Fori(0, NB) as b:
                with dve.If(b < nblk):
                    for g, name in enumerate(("HA", "HB")):
                        cols = slice(256 * g, 256 * g + 256)
                        dve.wait_ge(S["sg"], 2 * b + g + 1)
                        dve.tensor_tensor(W["sg"][:, cols], W["sg"][:, cols], bank[name][:, 0:256], ALU.mult)
                        dve.drain()
                        dve.tensor_tensor(h[:, cols], W["sg"][:, cols], bank[name][:, 256:512], ALU.mult).then_inc(S["h"], 1)
                    dve.wait_ge(S["blocks_done"], b + 2)
                    dve.wait_ge(S["y_out"], b * 16 + 16)
                    for n0 in range(2):
                        cols = slice(512 * n0, 512 * n0 + 512)
                        i = dve.tensor_tensor(W["ysb"][:, cols], bank[f"Y{n0}"][:, :], W["gt2"][:, cols], ALU.mult)
                    i.then_inc(S["y_read"], 1)


def combine(nc, S, V, W, dram):
    a = [W["slots"][:, 4 * D * b:4 * D * b + 4 * D] for b in range(2)]
    buf = [{n: split(a[b], 4)[:, i, :] for i, n in enumerate(("y0", "y1", "x1", "res"))} for b in range(2)]

    def run(eng, step):
        for t in range(2):
            step(t, t)
        with eng.Fori(1, NT // 2) as u:
            for b in range(2):
                step(2 * u + b, b)

    with nc.Block() as block:
        @block.sync
        def _(sp):
            def step(t, b):
                S.wait(sp, "summed", t - 1)
                sp.dma_start(buf[b]["x1"], dram["x1"][bass.ds(t * P, P), :]).then_inc(S[f"x1_in{b}"], 16)
            run(sp, step)

        @block.gpsimd
        def _(pool):
            def step(t, b):
                S.wait(pool, "summed", t - 1)
                for c in range(2):
                    pool.tensor_copy(W["idx_now2"][b][:, c:c + 1], W["dest"][:, bass.ds(2 * t + c, 1)])
                pool.drain()
                for c in range(2):
                    pool.indirect_dma_start(buf[b][f"y{c}"], None, dram["y"],
                                            bass.IndirectOffsetOnAxis(ap=W["idx_now2"][b][:, c:c + 1],
                                                                      axis=0)).then_inc(S[f"y_in{b}"], 16)
            run(pool, step)

        @block.vector
        def _(dve):
            def step(t, b):
                m = buf[b]
                S.wait(dve, f"x1_in{b}", 8 * (t - b) + 16)
                S.wait(dve, f"y_in{b}", 16 * (t - b) + 32)
                S.wait(dve, f"stored_out{b}", 8 * (t - b))
                dve.scalar_tensor_tensor(m["x1"], m["y0"], V["top_w"][:, bass.ds(2 * t, 1)], m["x1"], ALU.mult, ALU.add)
                dve.drain()
                dve.scalar_tensor_tensor(m["res"], m["y1"], V["top_w"][:, bass.ds(2 * t + 1, 1)], m["x1"], ALU.mult,
                                         ALU.add).then_inc(S["summed"], 1)
            run(dve, step)

        @block.scalar
        def _(act):
            def step(t, b):
                S.wait(act, "summed", t + 1)
                act.dma_start(dram["out"][bass.ds(t * P, P), :], buf[b]["res"]).then_inc(S[f"stored_out{b}"], 16)
            run(act, step)
            for b in range(2):
                act.wait_ge(S[f"stored_out{b}"], 8 * NT)


def program(nc, ins, out, nt=NT, stages=9):
    with ExitStack() as ctx:
        S = Sync(nc, ctx)
        ps = [ctx.enter_context(nc.psum_tensor(f"ps{i}", [P, 512], F32)) for i in range(8)]
        V, arena, total = views(nc, ctx)
        scratch = lambda n, shape, dt=F32: nc.dram_tensor(n, shape, dt, kind="Internal").ap()
        dram = {"x": ins["x"], "gates": scratch("gates", [P, 2 * D]), "mid": scratch("mid", [NT, P, NPK]),
                "x1": scratch("x1", [T, D]), "xn2": scratch("xn2", [T + 1, D]),
                "row_tok": scratch("row_tok", [(NB + 1) * P, 1], I32), "y": scratch("y", [NB * P, D]), "out": out}
        setup(nc, S, ps, V, ins, dram)
        pass1(nc, S, ps, V, dram, nt)
        W = views2(V, arena, total)
        pass2(nc, S, ps, V, W, ins, dram, nt)
        if stages < 3:
            return
        W = views3(V, arena, total)
        dispatch(nc, S, ps, V, W, ins, dram)
        experts(nc, S, ps, V, W, ins, dram)
        combine(nc, S, V, W, dram)


def host_arrays(inputs):
    a = {n: np.asarray(v) for n, v in inputs.items()}
    cols = np.zeros((P, NCOLS), np.float32)

    def col(name, v):
        v = v.reshape(-1)
        lo, hi = COLS[name]
        cols[:, lo:hi] = v.reshape(hi - lo, P).T

    mix = a["rwkv_shift_mix"].reshape(-1)
    col("mix", np.concatenate([mix[:3 * C + LORA_WA], np.zeros(P - LORA_WA, np.float32),
                               mix[3 * C + LORA_WA:], np.zeros(P - LORA_G, np.float32)]))
    for name, src in (("c", "c"), ("ada_b", "ada_b"), ("n1g", "norm1_g"), ("n2g", "norm2_g"), ("w0", "rwkv_w0"),
                      ("a0", "rwkv_a0"), ("k_k", "rwkv_k_k"), ("k_a", "rwkv_k_a"), ("r_k", "rwkv_r_k")):
        col(name, a[src])
    rows = np.concatenate([a[n].reshape(-1) for n in ("rwkv_ln_w", "rwkv_ln_b", "q_norm_g", "k_norm_g", "attn_sinks",
                                                      "router_grp_b", "router_exp_b")])[None, :]
    b = a["ada_b"].reshape(6, D)
    consts, onehot = shape_constants()
    return {"x": a["x"].reshape(T, D), "cols": cols, "rows": rows, "consts": consts, "onehot": onehot,
            "gate_b": np.concatenate([b[2], b[5]])[None, :],
            "ada_w": a["ada_w"][0], "w_in": a["w_in"][0], "w2": a["rwkv_w2"][0], "a2": a["rwkv_a2"][0],
            "g2": a["rwkv_g2"][0], "rel_bias": a["rel_bias"], "w_out": a["w_out"][0],
            "w_router": np.concatenate([a["router_grp_w"][0], a["router_exp_w"][0]], 1),
            "w1": a["exp_w1"][0], "w3": a["exp_w3"][0], "w2e": a["exp_w2"][0]}


def kernel(**inputs):
    import concourse.bacc as bacc
    from concourse.bass_utils import run_bass_kernel_spmd

    nc = bacc.Bacc("TRN2", target_bir_lowering=False, num_devices=1)
    arrays = {n: np.ascontiguousarray(v) for n, v in host_arrays(inputs).items()}
    ins = {n: nc.dram_tensor(n, v.shape, mybir.dt.from_np(v.dtype), kind="ExternalInput").ap() for n, v in arrays.items()}
    out = nc.dram_tensor("out", (T, D), F32, kind="ExternalOutput").ap()
    program(nc, ins, out)
    result = run_bass_kernel_spmd(nc, [arrays], core_ids=[0])
    return result.results[0]["out"].reshape(1, T, D)
```

```python
from contextlib import ExitStack

import numpy as np
import concourse.bass as bass
from concourse import mybir

F32 = mybir.dt.float32
I32 = mybir.dt.int32
U32 = mybir.dt.uint32
ALU = mybir.AluOpType
ACT = mybir.ActivationFunctionType
AX = mybir.AxisListType

D = 1024
T = 2048
P = 128
NT = T // P
KD = D // P
CHUNK = 64
HD = 64
C = 512
H = C // HD
CC = C // P
LORA_WA = 64
LORA_G = 96
RW_COLS = 3 * C + LORA_WA + LORA_G
QH, KVH = 8, 2
IN_COLS = RW_COLS + (QH + 2 * KVH) * HD
NF = 3 * CC + 2
LAMBDA = float(np.exp(-0.5))
NEG = -1e30
KEYS = 192
NG, EG, NE, FE = 4, 8, 32, 512
NR = NG + NE
NB = (2 * T + NE * (P - 1)) // P + 1
FULL_BLOCKS = 2 * T // P
LEVELS = (1, 2, 4, 8, 16, 32)

COLS = {}
_at = 0
for _n, _w in (("c", KD), ("ada_b", 48), ("n1g", KD), ("n2g", KD), ("mix", NF), ("w0", CC), ("a0", CC),
               ("k_k", CC), ("k_a", CC), ("r_k", CC)):
    COLS[_n] = (_at, _at + _w)
    _at += _w
NCOLS = _at
ROWS = {}
_at = 0
for _n, _w in (("ln_w", C), ("ln_b", C), ("q_g", HD), ("k_g", HD), ("sinks", QH), ("rb", NR)):
    ROWS[_n] = (_at, _at + _w)
    _at += _w
NROWS = _at
CONSTS = {}
_at = 0
for _n, _w in (("ident", P), ("scan", C), ("mmask", 4 * P), ("level", len(LEVELS) * P), ("headsel", 2),
               ("before", P), ("ones", P), ("iota_e", NE), ("group_e", NE), ("block_row", NB),
               ("token", NT), ("sel8", C)):
    CONSTS[_n] = (_at, _at + _w)
    _at += _w
NCONST = _at
PK = {}
_at = 0
for _n, _w in (("AR", 2 * C), ("BT", C), ("KT", C), ("A", C), ("B", C), ("K", C), ("V", C),
               ("gate", C), ("ya", C), ("PC", 8), ("bon", 8)):
    PK[_n] = (_at, _at + _w)
    _at += _w
NPK = _at


def shape_constants():
    k = np.zeros((P, NCONST), np.float32)
    j, t = np.arange(P)[:, None], np.arange(P)[None, :]

    def put(name, a):
        a0, a1 = CONSTS[name]
        k[:a.shape[0], a0:a1] = a

    put("ident", np.eye(P))
    put("scan", np.tile((np.arange(C) % CHUNK != 0)[None, :], (P, 1)))
    same = j // CHUNK == t // CHUNK
    strict, incl = same & (j < t), same & (j <= t)
    put("mmask", np.concatenate([strict, incl, strict, incl], 1))
    put("level", np.concatenate([(j // (2 * s) == t // (2 * s)) & (j // s % 2 == 0) & (t // s % 2 == 1)
                                 for s in LEVELS], 1))
    put("headsel", (np.arange(P)[:, None] // HD) == np.arange(2)[None, :])
    put("before", j < t)
    put("ones", np.ones((P, P)))
    put("iota_e", np.tile(np.arange(NE)[None], (P, 1)))
    put("group_e", np.tile(np.arange(NE)[None] // EG, (P, 1)))
    put("block_row", np.tile(P * np.arange(NB)[None], (P, 1)))
    put("token", np.arange(P)[:, None] + P * np.arange(NT)[None])
    ch = np.arange(C)
    put("sel8", (ch[None, :] // HD) == np.arange(8)[:, None])
    rel = np.arange(2 * CHUNK)[None, :] - CHUNK - np.arange(CHUNK)[:, None]
    n = np.abs(rel)
    nf = np.maximum(n, 1).astype(np.float32)
    large = 8 + (np.log(nf / np.float32(8)) / np.float32(np.log(16.0)) * np.float32(8)).astype(np.int32)
    bucket = np.where(rel > 0, 16, 0) + np.where(n < 8, n, np.minimum(large, 15))
    onehot = (np.arange(32)[:, None, None] == bucket[None]).astype(np.float32)
    return k, onehot.reshape(32, 2 * CHUNK * CHUNK)


USES1 = {"A0": ("r", "v", "q"), "A1": ("k", "lora", "kv"),
         "T0": ("xT", "qT", "tokA", "tokK", "P0", "P1"), "T1": ("xT", "kT", "tokB", "tokV", "P0", "P1"),
         "C0": ("zw", "nbc", "L0", "L1"), "C1": ("za", "L0", "L1"),
         "C2": ("gate",), "C3": ("ssn", "nT", "bon")}
BANK1 = {b: i for i, b in enumerate(USES1)}
IN_GROUPS = {"r": ("A0", 0), "k": ("A1", 1), "v": ("A0", 2), "lora": ("A1", 3)}


class Sync:

    def __init__(self, nc, ctx):
        self.nc, self.ctx, self.sems = nc, ctx, {}

    def __getitem__(self, name):
        if name not in self.sems:
            self.sems[name] = self.ctx.enter_context(self.nc.semaphore("s_" + name))
        return self.sems[name]

    def wait(self, eng, name, value):
        if isinstance(value, int) and value <= 0:
            return
        eng.wait_ge(self[name], value)


class Banks:

    def __init__(self, sync, prefix, uses, nt, ahead=()):
        self.sync, self.prefix, self.uses, self.nt, self.ahead = sync, prefix, uses, nt, ahead

    def _nth(self, bank, use, t):
        uses = self.uses[bank]
        early = [u for u in uses if u in self.ahead]
        at = uses.index(use)
        if use in early:
            return early.index(use) if isinstance(t, int) and t == 0 else len(early) + len(uses) * (t - 1) + at
        if isinstance(t, int) and t == self.nt - 1:
            at -= sum(u in early for u in uses[:at])
        return len(early) + len(uses) * t + at

    def wait_free(self, pe, bank, use, t):
        self.sync.wait(pe, f"{self.prefix}{bank}_free", self._nth(bank, use, t))

    def full(self, ins, bank):
        ins.then_inc(self.sync[f"{self.prefix}{bank}_full"], 1)

    def wait_full(self, eng, bank, use, t):
        if isinstance(t, int) and t < 0:
            return
        self.sync.wait(eng, f"{self.prefix}{bank}_full", self._nth(bank, use, t) + 1)

    def free(self, ins, bank):
        ins.then_inc(self.sync[f"{self.prefix}{bank}_free"], 1)

    def wait_read(self, eng, bank, use, t):
        if isinstance(t, int) and t < 0:
            return
        self.sync.wait(eng, f"{self.prefix}{bank}_free", self._nth(bank, use, t) + 1)


class Arena:

    def __init__(self, tensor, at=0):
        self.tensor, self.at = tensor, at

    def take(self, width):
        a = self.tensor[:, self.at:self.at + width]
        self.at += width
        return a


def split(ap, a):
    return ap.rearrange("p (a b) -> p a b", a=a)


def per_channel(col, n):
    p, k = col.shape
    return col.unsqueeze(2).to_broadcast([p, k, n])


def setup(nc, S, ps, V, ins, dram):
    ada = V["ada_slots"]
    pieces = [0, 1, 2, 3, 6, 7, 8, 9, 4, 5, 10, 11]
    ada_v = ins["ada_w"].rearrange("(k p) n -> p k n", p=P)
    w_in_v = ins["w_in"].rearrange("(k p) n -> p k n", p=P)
    col = V["col"]
    ident = V["k"]("ident")
    nb = 2 * CHUNK * CHUNK // 512
    with nc.Block() as block:
        @block.sync
        def _(sp):
            sp.dma_start(V["cols"], ins["cols"]).then_inc(S["params"], 16)
            sp.dma_start(V["rows"], ins["rows"].to_broadcast([P, NROWS])).then_inc(S["params"], 16)
            sp.dma_start(V["rel_bias"][0:32, :], ins["rel_bias"]).then_inc(S["params"], 16)
            sp.dma_start(V["consts"], ins["consts"]).then_inc(S["params"], 16)
            sp.wait_ge(S["params"], 64)
            sp.dma_start(V["onehot"][0:32, :], ins["onehot"]).then_inc(S["onehot"], 16)
            for n, piece in enumerate(pieces):
                if n >= 2:
                    sp.wait_ge(S["ada_used"], n - 1)
                sp.dma_start(ada[n % 2], ada_v[:, :, 512 * piece:512 * piece + 512]).then_inc(S[f"ada_in{n % 2}"], 16)
                if n >= 2 and n - 2 < KD:
                    sp.dma_start(V["w_in"][:, n - 2, :], w_in_v[:, n - 2, :]).then_inc(S["w_in"], 16)
                if n == 6:
                    sp.wait_ge(S["bias_mm"], nb)
                    sp.wait_ge(S["bias_copied"], nb)
                    sp.dma_start(dram["bias"], V["bias_sb"][0:QH, :]).then_inc(S["bias_out"], 16)
                    sp.dma_start(V["gt"], ins["gate_b"].to_broadcast([P, 2 * D])).then_inc(S["gate_b"], 16)
            back = dram["bias"].rearrange("h (i j) -> i h j", i=CHUNK)
            sp.wait_ge(S["bias_out"], 16)
            sp.wait_ge(S["bias_fill"], 1)
            for dst, lo, hi in ((V["bias_first"][0:64], 0, 64), (V["bias_v"][0:64, :, 64:128], 64, 128),
                                (V["bias_v"][64:128, :, 64:192], 0, 128)):
                sp.dma_start(dst, back[:, :, lo:hi]).then_inc(S["bias_in"], 16)
            sp.dma_start(V["w2"][0:32, :], ins["w2"]).then_inc(S["params"], 16)
            sp.dma_start(V["w2"][32:64, :], ins["a2"]).then_inc(S["params"], 16)
            sp.dma_start(V["g2"][0:LORA_G, :], ins["g2"]).then_inc(S["params"], 16)
            sp.wait_ge(S["rows_done"], 1)
            sp.dma_start(dram["gates"], V["gt"]).then_inc(S["gates_out"], 16)
            sp.wait_ge(S["gates_out"], 16)
            sp.wait_ge(S["bias_in"], 48)
            sp.wait_ge(S["w_in"], 16 * KD)
            sp.wait_ge(S["params"], 112)

        @block.scalar
        def _(act):
            act.wait_ge(S["params"], 64)
            act.activation(V["csig"], col("c"), ACT.Sigmoid).then_inc(S["csig"], 1)
            for i in range(nb):
                act.wait_ge(S["bias_mm"], i + 1)
                act.activation(V["bias_sb"][0:QH, 512 * i:512 * i + 512], ps[i % 2][0:QH, :],
                               ACT.Copy).then_inc(S["bias_copied"], 1)

        @block.tensor
        def _(pe):
            pe.wait_ge(S["onehot"], 16)
            pe.wait_ge(S["cs"], 2)

            def bias(i):
                if i >= 2:
                    pe.wait_ge(S["bias_copied"], i - 1)
                pe.matmul(ps[i % 2][0:QH, :], V["rel_bias"][0:32, :], V["onehot"][0:32, 512 * i:512 * i + 512],
                          start=True, stop=True).then_inc(S["bias_mm"], 1)

            for n in range(len(pieces)):
                if n < 4:
                    for i in range(4):
                        bias(4 * n + i)
                pe.wait_ge(S[f"ada_in{n % 2}"], 16 * (n // 2 + 1))
                if n >= 3:
                    pe.wait_ge(S["mod_read"], n - 2)
                for k in range(KD):
                    mm = pe.matmul(ps[2 + n % 3][:, :], V["cs_rows"][:, k, :], ada[n % 2][:, k, :],
                                   start=(k == 0), stop=(k == KD - 1))
                mm.then_inc(S["ada_used"], 1)
                if 1 <= n <= 8:
                    pe.wait_ge(S["mod_read"], n)
                    for i in range(4):
                        tp = pe.transpose(ps[5 + n % 3][:, P * i:P * i + P], V["mod"][n % 2][:, P * i:P * i + P], ident)
                    tp.then_inc(S["mod_T"], 1)

        @block.gpsimd
        def _(pool):
            pool.memset(V["bias"], NEG).then_inc(S["bias_fill"], 1)
            for name in ("raw", "qkv1", "Pm", "kT"):
                pool.memset(V[name], 0.0)
            pool.memset(V["minus_half"], -0.5)
            pool.memset(V["Pb"], 1.0)
            pool.memset(V["S"], 0.0)

        @block.vector
        def _(dve):
            dve.wait_ge(S["csig"], 1)
            dve.tensor_tensor(V["cs"], V["csig"], col("c"), ALU.mult).then_inc(S["cs"], 1)
            dve.drain()
            dve.tensor_copy(V["cs_rows"], per_channel(V["cs"], P)).then_inc(S["cs"], 1)
            dve.tensor_tensor(V["rksel"], per_channel(col("r_k"), 2),
                              V["k"]("headsel").unsqueeze(1).to_broadcast([P, CC, 2]), ALU.mult)
            dve.tensor_scalar(V["omka"], col("k_a"), -1.0, 1.0, ALU.mult, ALU.add)
            ab = COLS["ada_b"][0]
            for n in range(len(pieces) + 1):
                if n < 8:
                    dve.wait_ge(S["ada_used"], n + 1)
                    dve.tensor_copy(V["mod"][(n + 1) % 2], ps[2 + n % 3][:, :]).then_inc(S["mod_read"], 1)
                elif n < len(pieces):
                    dve.wait_ge(S["ada_used"], n + 1)
                    dve.wait_ge(S["gate_b"], 16)
                    cols = slice(512 * (n - 8), 512 * (n - 8) + 512)
                    dve.tensor_tensor(V["gt"][:, cols], ps[2 + n % 3][:, :], V["gt"][:, cols], ALU.add).then_inc(
                        S["mod_read"], 1)
                if 1 <= n <= 8:
                    dve.wait_ge(S["mod_T"], n)
                    name, b0 = (("b1", 0), ("s1", 8), ("b2", 24), ("s2", 32))[(n - 1) // 2]
                    at = 4 * ((n - 1) % 2)
                    dve.tensor_tensor(V[name][:, at:at + 4].unsqueeze(2), split(ps[5 + n % 3][:, :], 4)[:, :, 0:1],
                                      V["cols"][:, ab + b0 + at:ab + b0 + at + 4].unsqueeze(2), ALU.add)
            dve.drain()
            for s, g in (("s1", "n1g"), ("s2", "n2g")):
                dve.scalar_tensor_tensor(V[s], V[s], 1.0, col(g), ALU.add, ALU.mult)
            dve.engine_nop().then_inc(S["rows_done"], 1)


def load_pack(eng, S, W, dram, n, b):
    eng.dma_start(W[f"pk{b}"], dram["mid"][bass.ds(n, 1)].rearrange("a p n -> (a p) n")).then_inc(S[f"pack{b}"], 16)


def pass1(nc, S, ps, V, W, ins, dram, nt):
    B = Banks(S, "a", USES1, nt, ahead=("xT", "r", "k", "v", "lora", "q", "kv"))
    bank = {b: ps[i] for b, i in BANK1.items()}
    k, col, row, pk = V["k"], V["col"], V["row"], V["pk"]
    ident = k("ident")
    heads4 = lambda h: (64 * (h % 2), h // 2)

    ORDER = (("xT", 1), ("x", 2), ("lora1", 0), ("kk", 0), ("att1", 0), ("in_r1", 1), ("in_r2", 1), ("ew1", 0),
             ("in_k1", 1), ("ev_r", 1), ("ew2", 0), ("in_k2", 1), ("nbc", 0), ("att2", 0), ("in_v1", 1), ("in_v2", 1),
             ("ev_k", 1),
             ("ew3", 0), ("att3_0", 0), ("in_wa", 1),
             ("tok1", 0), ("exp_0", 0), ("in_g", 1), ("ev_v", 1), ("tok2", 0), ("att3_1", 0), ("exp_1", 0),
             ("in_q1", 1), ("att4_0", 0), ("in_q2", 1), ("att5_0", 0), ("ev_lora", 1), ("norm", 2),
             ("att4_1", 0), ("lora0", 1), ("in_kv", 1), ("ev_q", 1), ("att5_1", 0), ("out", 0), ("ev_kv", 1))

    def run(eng, steps):
        def tile(t, parity, front=True, back=True):
            for name, ahead in ORDER:
                if (front if ahead else back) and name in steps:
                    steps[name](t + ahead, (parity + ahead) % 2)

        tile(-1, 1, back=False)
        tile(0, 0)
        tile(1, 1)
        if nt > 4:
            with eng.Fori(1, nt // 2 - 1) as u:
                tile(2 * u, 0)
                tile(2 * u + 1, 1)
        tile(nt - 2, 0)
        tile(nt - 1, 1, front=False)

    with nc.Block() as block:
        @block.sync
        def _(sp):
            def load_x(n, b):
                if isinstance(n, int) and n >= nt:
                    return
                B.wait_full(sp, "T1", "xT", n - 1)
                sp.dma_start(V["x"], dram["x"][bass.ds(n * P, P), :]).then_inc(S["x"], 16)

            def store(t, b):
                S.wait(sp, "ya", t + 1)
                sp.sem_inc(S["sp_passed"], 1)
                B.wait_read(sp, "T0", "tokK", t)
                sp.dma_start(dram["mid"][bass.ds(t, 1)].rearrange("a p n -> (a p) n"), V["pk_all"]).then_inc(S["stored"], 16)
                if isinstance(t, int) and t == nt - 2:
                    B.wait_full(sp, "A1", "kv", nt - 1)
                    sp.wait_ge(S["stored"], 16 * (nt - 1))
                    for n in range(2):
                        load_pack(sp, S, W, dram, n, n)
                    sp.dma_start(W["w_router"], ins["w_router"].rearrange("(k p) n -> p k n", p=P)).then_inc(S["w_out"], 16)
                    sp.dma_start(W["gt1"], dram["gates"][:, 0:D]).then_inc(S["w_out"], 16)

            load_x(0, 0)
            sp.dma_start(dram["xn2"][T:T + 1, :].rearrange("o (a n) -> (o a) n", a=4),
                         V["S"][0:4, :]).then_inc(S["zero_row"], 16)
            run(sp, {"x": load_x, "out": store})
            sp.wait_ge(S["zero_row"], 16)
            sp.wait_ge(S["stored"], 16 * nt)

        @block.tensor
        def _(pe):
            def xT(n, b):
                S.wait(pe, "xn", n + 1)
                for half, name in enumerate(("T0", "T1")):
                    B.wait_free(pe, name, "xT", n)
                    for i in range(4):
                        c = 4 * half + i
                        mm = pe.transpose(bank[name][:, P * i:P * i + P], V["x"][:, P * c:P * c + P], ident)
                    B.full(mm, name)

            def in_group(g, part):
                name, index = IN_GROUPS[g]

                def go(n, b):
                    if part == 0:
                        B.wait_read(pe, "T1", "xT", n)
                        B.wait_free(pe, name, g, n)
                    parts = [(P * c, P, C * index + P * c) for c in (2 * part, 2 * part + 1)]
                    if g == "lora":
                        parts = [[(0, LORA_WA, 3 * C)], [(P, LORA_G, 3 * C + LORA_WA)]][part]
                    for at, m, w0 in parts:
                        for kk in range(KD):
                            mm = pe.matmul(bank[name][0:m, at:at + P], V["w_in"][:, kk, w0:w0 + m], V["hT"][:, kk, :],
                                           start=(kk == 0), stop=(kk == KD - 1))
                    if part == 1:
                        B.full(mm, name)
                return go

            def in_tok(g, name, w0, w, ks=range(KD)):
                def go(n, b):
                    if ks[0] == 0:
                        B.wait_free(pe, name, g, n)
                    for kk in ks:
                        mm = pe.matmul(bank[name][:, 0:w], V["hT"][:, kk, :], V["w_in"][:, kk, w0:w0 + w],
                                       start=(kk == 0), stop=(kk == KD - 1))
                    if ks[-1] == KD - 1:
                        B.full(mm, name)
                return go

            def lora1(t, b):
                S.wait(pe, "lora_in", t + 1)
                B.wait_free(pe, "C0", "zw", t)
                for c in range(CC):
                    mm = pe.matmul(bank["C0"][:, P * c:P * c + P], V["w2"][0:32, P * c:P * c + P], V["tw"][0:32, :],
                                   start=True, stop=True)
                B.full(mm, "C0")
                B.wait_free(pe, "C1", "za", t)
                for c in range(CC):
                    mm = pe.matmul(bank["C1"][:, P * c:P * c + P], V["w2"][32:64, P * c:P * c + P],
                                   V["f"][b][32:64, 3 * CC, :], start=True, stop=True)
                B.full(mm, "C1")
                B.wait_free(pe, "C2", "gate", t)
                S.wait(pe, "ya", t)
                mm = pe.matmul(bank["C2"][:, :], V["sg"][0:LORA_G, :], V["g2"][0:LORA_G, :], start=True, stop=True)
                B.full(mm, "C2")

            def ew1(t, b):
                S.wait(pe, "sq", t + 1)
                B.wait_free(pe, "C3", "ssn", t)
                for c in range(CC):
                    mm = pe.matmul(bank["C3"][:, 2 * c:2 * c + 2], V["sq"][:, P * c:P * c + P], k("headsel"),
                                   start=True, stop=True)
                B.full(mm, "C3")

            def ew2(t, b):
                S.wait(pe, "ninv", t + 1)
                B.wait_free(pe, "C3", "nT", t)
                B.full(pe.transpose(bank["C3"][0:8, 0:P], V["ninv"], ident), "C3")

            def nbc(t, b):
                B.wait_read(pe, "C3", "nT", t)
                B.wait_free(pe, "C0", "nbc", t)
                for c in range(CC):
                    mm = pe.matmul(bank["C0"][:, P * c:P * c + P], k("sel8")[0:8, P * c:P * c + P], V["nT"][0:8, :],
                                   start=True, stop=True)
                B.full(mm, "C0")

            def tok(uses):
                def go(t, b):
                    S.wait(pe, "ew3", t + 1)
                    src = {"tokA": lambda c: pk["AR_v"][:, c, 0, :], "tokB": lambda c: split(pk["BT"], 4)[:, c, :],
                           "tokK": lambda c: split(pk["KT"], 4)[:, c, :], "tokV": lambda c: V["f"][b][:, 2 * CC + c, :]}
                    for use, name in uses:
                        B.wait_free(pe, name, use, t)
                        for c in range(CC):
                            mm = pe.transpose(bank[name][:, P * c:P * c + P], src[use](c), ident)
                        B.full(mm, name)
                    if uses[0][0] == "tokA":
                        return
                    S.wait(pe, "rk", t + 1)
                    B.wait_free(pe, "C3", "bon", t)
                    for c in range(CC):
                        mm = pe.matmul(bank["C3"][:, 2 * c:2 * c + 2], V["rk"][:, P * c:P * c + P], V["rksel"][:, c, :],
                                       start=True, stop=True)
                    B.full(mm, "C3")
                return go

            def att2(t, b):
                S.wait(pe, "qn", t + 1)
                for name, use, n, base in (("T0", "qT", 4, 0), ("T1", "kT", 2, C)):
                    B.wait_free(pe, name, use, t)
                    for i in range(n):
                        mm = pe.transpose(bank[name][:, P * i:P * i + P], V["qn"][:, base + P * i:base + P * i + P], ident)
                    B.full(mm, name)

            def att3(g):
                def go(t, b):
                    B.wait_read(pe, "T0", "qT", t)
                    B.wait_read(pe, "T1", "kT", t)
                    for i in range(4):
                        h = 4 * g + i
                        hp, c = heads4(h)
                        name = f"C{i % 2}"
                        if i < 2:
                            B.wait_free(pe, name, f"L{g}", t)
                        mm = pe.matmul(bank[name][:, KEYS * (i // 2):KEYS * (i // 2) + KEYS],
                                       V["qT"][hp:hp + 64, P * c:P * c + P], V["kT_v"][hp:hp + 64, g, :],
                                       start=True, stop=True)
                        if i >= 2:
                            B.full(mm, name)
                return go

            def att4(g):
                def go(t, b):
                    S.wait(pe, "probs", 2 * t + g + 1)
                    for half, name in enumerate(("T0", "T1")):
                        B.wait_free(pe, name, f"P{g}", t)
                        for i in range(2):
                            for part in range(2):
                                mm = pe.transpose(bank[name][:, 256 * i + P * part:256 * i + P * part + P],
                                                  V["Pm_v"][:, 2 * half + i, P * part:P * part + P], ident)
                        B.full(mm, name)
                return go

            def att5(g):
                def go(t, b):
                    B.wait_read(pe, "C2", "gate", t)
                    for i in range(4):
                        h = 4 * g + i
                        B.wait_read(pe, f"T{i // 2}", f"P{g}", t)
                        for part in range(2):
                            v = V["qkv"][b if part else 1 - b][:, 640 + 64 * g:704 + 64 * g]
                            mm = pe.matmul(bank["C2"][:, 64 * h:64 * h + 64], V["PT"][:, i, P * part:P * part + P], v,
                                           start=(part == 0), stop=(part == 1))
                    mm.then_inc(S["pv"], 1)
                return go

            run(pe, {"xT": xT, **{f"in_{g}{part + 1}": in_group(g, part) for g in "rkv" for part in range(2)},
                     "in_wa": in_group("lora", 0), "in_g": in_group("lora", 1),
                     "in_q1": in_tok("q", "A0", RW_COLS, C, range(0, 4)), "in_q2": in_tok("q", "A0", RW_COLS, C, range(4, KD)),
                     "in_kv": in_tok("kv", "A1", RW_COLS + C, 2 * P), "lora1": lora1, "ew1": ew1, "ew2": ew2, "nbc": nbc,
                     "tok1": tok((("tokA", "T0"), ("tokB", "T1"))), "tok2": tok((("tokK", "T0"), ("tokV", "T1"))),
                     "att2": att2, "att3_0": att3(0), "att3_1": att3(1), "att4_0": att4(0), "att4_1": att4(1),
                     "att5_0": att5(0), "att5_1": att5(1)})

        @block.scalar
        def _(act):
            def norm(n, b):
                if isinstance(n, int) and n >= nt:
                    return
                S.wait(act, "x", 16 * n + 16)
                S.wait(act, "ms10", n - 1)
                act.activation(V["junk"], V["x"], ACT.Square, accum_out=V["ssx"]).then_inc(S["ssx"], 1)

            def xT(n, b):
                for half, name in enumerate(("T0", "T1")):
                    B.wait_full(act, name, "xT", n)
                    if half == 0:
                        B.wait_full(act, "A1", "kv", n - 1)
                    for i in range(4):
                        c = 4 * half + i
                        a = act.activation(V["hT"][:, c, :], bank[name][:, P * i:P * i + P], ACT.Identity,
                                           scale=V["s1"][:, c:c + 1], bias=V["b1"][:, c:c + 1])
                        if i == 3:
                            B.free(a, name)

            def ev(g):
                name, index = IN_GROUPS[g]

                def go(n, b):
                    B.wait_full(act, name, g, n)
                    S.wait(act, "feat", 4 * (n - 1) + index + 1)
                    S.wait(act, "hist", 4 * (n - 1) + index + 1)
                    if g == "lora":
                        act.activation(V["raw_v"][0:LORA_WA, 12, 1:P + 1], bank[name][0:LORA_WA, 0:P], ACT.Copy)
                        a = act.activation(V["raw_v"][0:LORA_G, 13, 1:P + 1], bank[name][0:LORA_G, P:2 * P], ACT.Copy)
                    else:
                        a = act.activation(V["raw_v"][:, 4 * index:4 * index + 4, 1:P + 1],
                                           split(bank[name][:, :], 4), ACT.Copy)
                    B.free(a, name)
                return go

            def ev_q(n, b):
                B.wait_full(act, "A0", "q", n)
                B.free(act.activation(V["qkv"][b][:, 0:C], bank["A0"][:, :], ACT.Copy), "A0")

            def ev_kv(n, b):
                B.wait_full(act, "A1", "kv", n)
                S.wait(act, "pv", 2 * n)
                B.free(act.activation(V["qkv"][b][:, C:768], bank["A1"][:, 0:2 * P], ACT.Copy), "A1")

            def lora1(t, b):
                S.wait(act, "feat", 4 * t + 4)
                B.wait_full(act, "C2", "gate", t - 1)
                act.activation(V["tw"][0:32, :], V["f"][b][0:32, 12, :], ACT.Tanh)
                act.activation(V["sg"][0:LORA_G, :], V["f"][b][0:LORA_G, 13, :], ACT.Sigmoid).then_inc(S["lora_in"], 1)

            def kk(t, b):
                S.wait(act, "kkr", t + 1)
                B.wait_full(act, "C3", "bon", t - 1)
                act.activation(V["sq"], V["kk"], ACT.Square).then_inc(S["sq"], 1)

            def ew1(t, b):
                S.wait(act, "ew3", t)
                for name, use, out, bias in (("C0", "zw", "sw", "w0"), ("C1", "za", "sa", "a0")):
                    B.wait_full(act, name, use, t)
                    for c in range(CC):
                        a = act.activation(V[out][:, P * c:P * c + P], bank[name][:, P * c:P * c + P], ACT.Sigmoid,
                                           bias=col(bias)[:, c:c + 1])
                    B.free(a, name)
                S.wait(act, "stored", 16 * t)
                B.wait_full(act, "C2", "gate", t)
                B.free(act.activation(pk["gate"], bank["C2"][:, :], ACT.Copy), "C2")

            def ew2(t, b):
                S.wait(act, "cum", t + 1)
                act.activation(V["Pb_v"][:, :, 1:65], split(V["cum"], 8), ACT.Exp, scale=-LAMBDA)
                act.activation(V["Pinv"], V["cum"], ACT.Exp, scale=LAMBDA).then_inc(S["decay"], 1)

            def tok(use):
                def go(t, b):
                    B.wait_full(act, "T0", use, t)
                    B.free(act.activation(pk[use[3]], bank["T0"][:, :], ACT.Copy), "T0")
                return go

            def att1(t, b):
                act.drain()
                B.wait_read(act, "A1", "kv", t)
                act.activation(V["sqk"], V["qkv"][b][:, 0:640], ACT.Square).then_inc(S["sqk"], 1)

            def att2(t, b):
                B.wait_full(act, "T0", "qT", t)
                B.free(act.activation(V["qT"], bank["T0"][:, :], ACT.Copy), "T0")
                B.wait_full(act, "T1", "kT", t)
                B.free(act.activation(V["kT_v"][:, :, 64:KEYS], split(bank["T1"][:, 0:256], 2), ACT.Copy), "T1")

            def att3(g):
                def go(t, b):
                    S.wait(act, "negm", 2 * t + g + 1)
                    B.wait_full(act, "T1", "P1" if g == 0 else "P0", t - 1 + g)
                    for i in range(4):
                        h = 4 * g + i
                        act.activation(V["Pm_v"][:, i, 64:256], V["L"][:, i, :], ACT.Exp,
                                       bias=V["negm"][:, h:h + 1], accum_out=V["sm"][:, h:h + 1])
                    act.activation(V["es"][:, 4 * g:4 * g + 4], V["sd"][:, 4 * g:4 * g + 4], ACT.Exp).then_inc(S["probs"], 1)
                    if g == 1:
                        act.activation(V["kT_v"][:, :, 0:64], V["kT_v"][:, :, 128:192], ACT.Copy)
                        act.drain()
                return go

            def att4(g):
                def go(t, b):
                    B.wait_full(act, "T0", f"P{g}", t)
                    S.wait(act, "pv", 2 * t + g)
                    B.free(act.activation(V["PT"][:, 0:2, :], split(bank["T0"][:, :], 2), ACT.Copy), "T0")
                return go

            norm(0, 0)
            run(act, {"norm": norm, "xT": xT, "ev_r": ev("r"), "ev_k": ev("k"), "ev_v": ev("v"), "ev_lora": ev("lora"),
                      "ev_q": ev_q, "ev_kv": ev_kv, "lora0": lora1, "kk": kk, "ew1": ew1, "ew2": ew2, "tok1": tok("tokA"),
                      "tok2": tok("tokK"), "att1": att1,
                      "att2": att2, "exp_0": att3(0), "exp_1": att3(1), "att4_0": att4(0), "att4_1": att4(1)})

        @block.gpsimd
        def _(pool):
            def norm(n, b):
                if isinstance(n, int) and n >= nt:
                    return
                S.wait(pool, "msx", n + 1)
                pool.tensor_tensor(V["rsx"], V["msx"], V["minus_half"][:, 0:1], ALU.pow).then_inc(S["rsx"], 1)

            def ev(g):
                name, index = IN_GROUPS[g]
                m = LORA_G if g == "lora" else P
                c0, c1 = (12, 14) if g == "lora" else (4 * index, 4 * index + 4)

                def go(n, b):
                    B.wait_read(pool, name, g, n)
                    S.wait(pool, "feat", 4 * n + index)
                    raw = V["raw_v"]
                    pool.tensor_tensor(V["delta"][0:m, 0:c1 - c0, :], raw[0:m, c0:c1, 0:P], raw[0:m, c0:c1, 1:P + 1],
                                       ALU.subtract).then_inc(S["delta"], 1)
                    pool.drain()
                    pool.tensor_copy(raw[0:m, c0:c1, 0:1], raw[0:m, c0:c1, P:P + 1]).then_inc(S["hist"], 1)
                return go

            def att1(t, b):
                S.wait(pool, "ms10", t + 1)
                pool.tensor_tensor(V["rs10"], V["ms10"], V["minus_half"], ALU.pow).then_inc(S["rs10"], 1)

            def ew1(t, b):
                B.wait_read(pool, "C3", "ssn", t)
                pool.tensor_tensor(V["ninv"], V["ssm"], V["minus_half"][:, 0:8], ALU.pow).then_inc(S["ninv"], 1)

            def ew3(t, b):
                S.wait(pool, "kp", t + 1)
                B.wait_full(pool, "C3", "bon", t - 1)
                pool.tensor_tensor(V["rk"], V["f"][b][:, 0:4, :].rearrange("p c n -> p (c n)"), V["kp"],
                                   ALU.mult).then_inc(S["rk"], 1)

            norm(0, 0)
            run(pool, {"norm": norm, "ev_r": ev("r"), "ev_k": ev("k"), "ev_v": ev("v"), "ev_lora": ev("lora"),
                       "att1": att1, "ew1": ew1, "ew3": ew3})

        @block.vector
        def _(dve):
            def norm(n, b):
                if isinstance(n, int) and n >= nt:
                    return
                S.wait(dve, "ssx", n + 1)
                dve.tensor_scalar(V["msx"], V["ssx"], 1.0 / D, 1e-6, ALU.mult, ALU.add).then_inc(S["msx"], 1)
                S.wait(dve, "rsx", n + 1)
                dve.tensor_scalar(V["x"], V["x"], V["rsx"][:, 0:1], None, ALU.mult).then_inc(S["xn"], 1)

            def ev(g):
                name, index = IN_GROUPS[g]
                m = LORA_G if g == "lora" else P
                c0, c1 = (12, 14) if g == "lora" else (4 * index, 4 * index + 4)

                def go(n, b):
                    S.wait(dve, "delta", 4 * n + index + 1)
                    for c in range(c0, c1):
                        i = dve.scalar_tensor_tensor(V["f"][b][0:m, c, :], V["delta"][0:m, c - c0, :],
                                                     col("mix")[0:m, c:c + 1], V["raw_v"][0:m, c, 1:P + 1],
                                                     ALU.mult, ALU.add)
                    i.then_inc(S["feat"], 1)
                return go

            def att1(t, b):
                S.wait(dve, "sqk", t + 1)
                dve.tensor_reduce(V["ms10"], split(V["sqk"], 10), AX.X, ALU.add)
                dve.drain()
                dve.tensor_scalar(V["ms10"], V["ms10"], 1.0 / HD, 1e-6, ALU.mult, ALU.add).then_inc(S["ms10"], 1)
                S.wait(dve, "rs10", t + 1)
                B.wait_full(dve, "T1", "kT", t - 1)
                qk = V["qkv"][b]
                qn = split(V["qn"][:, 0:C], QH)
                kn = V["qn"][:, C:C + 256].rearrange("p (a e n) -> p a e n", a=2, e=2)
                dve.tensor_tensor(qn, split(qk[:, 0:C], QH), per_channel(V["rs10"][:, 0:8], HD), ALU.mult)
                dve.tensor_tensor(split(V["kn"], 2), split(qk[:, C:C + P], 2), per_channel(V["rs10"][:, 8:10], HD), ALU.mult)
                dve.drain()
                dve.tensor_tensor(qn, qn, row("q_g").unsqueeze(1).to_broadcast([P, QH, HD]), ALU.mult)
                kg = row("k_g").unsqueeze(1).to_broadcast([P, 2, HD])
                dve.tensor_tensor(kn[:, :, 0, :], split(V["kn"], 2), kg, ALU.mult)
                dve.tensor_tensor(kn[:, :, 1, :], split(V["kn"], 2), kg, ALU.mult).then_inc(S["qn"], 1)

            def kk(t, b):
                fk = V["f"][b][:, CC:2 * CC, :]
                dve.tensor_tensor(split(V["kk"], CC), fk, per_channel(col("k_k"), P), ALU.mult).then_inc(S["kkr"], 1)

            def ew1(t, b):
                B.wait_full(dve, "C3", "ssn", t)
                B.free(dve.tensor_scalar(V["ssm"], bank["C3"][:, 0:8], 1e-24, None, ALU.max), "C3")

            def ew2(t, b):
                B.wait_read(dve, "C0", "zw", t)
                dve.tensor_tensor_scan(V["cum"], k("scan"), V["sw"], 0.0, ALU.mult, ALU.add).then_inc(S["cum"], 1)
                B.wait_full(dve, "C3", "nT", t)
                B.free(dve.tensor_copy(V["nT"][0:8, :], bank["C3"][0:8, 0:P]), "C3")
                B.wait_full(dve, "C0", "nbc", t)
                S.wait(dve, "sq", t + 1)
                B.free(dve.scalar_tensor_tensor(V["kk"], V["kk"], -1.0, bank["C0"][:, :], ALU.mult, ALU.mult), "C0")

            def ew3(t, b):
                f = V["f"][b]
                B.wait_read(dve, "C1", "za", t)
                for c in range(CC):
                    dve.tensor_scalar(V["kp"][:, P * c:P * c + P], V["sa"][:, P * c:P * c + P], col("k_a")[:, c:c + 1],
                                      V["omka"][:, c:c + 1], ALU.mult, ALU.add)
                dve.drain()
                S.wait(dve, "stored", 16 * t)
                dve.scalar_tensor_tensor(V["bb"], V["kk"], -1.0, V["sa"], ALU.mult, ALU.mult)
                dve.tensor_tensor(split(V["kp"], CC), split(V["kp"], CC), f[:, CC:2 * CC, :], ALU.mult).then_inc(S["kp"], 1)
                S.wait(dve, "decay", t + 1)
                Pb, AR = V["Pb_v"], pk["AR_v"]
                q4 = lambda ap: ap.rearrange("p c (q n) -> p c q n", q=2)
                dve.tensor_tensor(q4(AR[:, :, 0, :]), V["kk"].rearrange("p (c q n) -> p c q n", c=CC, q=2),
                                  Pb[:, :, 0:64].rearrange("p (c q) n -> p c q n", q=2), ALU.mult)
                dve.tensor_tensor(q4(AR[:, :, 1, :]), q4(f[:, 0:CC, :]),
                                  Pb[:, :, 1:65].rearrange("p (c q) n -> p c q n", q=2), ALU.mult)
                dve.drain()
                dve.tensor_tensor(pk["BT"], V["bb"], V["Pinv"], ALU.mult)
                dve.tensor_tensor(pk["KT"], V["kp"], V["Pinv"], ALU.mult)
                dve.tensor_copy(pk["PC"].unsqueeze(2), Pb[:, :, 64:65]).then_inc(S["ew3"], 1)

            def tok(use):
                def go(t, b):
                    B.wait_full(dve, "T1", use, t)
                    B.free(dve.tensor_copy(pk[use[3]], bank["T1"][:, :]), "T1")
                    if use == "tokB":
                        return
                    B.wait_full(dve, "C3", "bon", t)
                    B.free(dve.tensor_copy(pk["bon"], bank["C3"][:, 0:8]), "C3")
                return go

            def att3(g):
                def go(t, b):
                    S.wait(dve, "probs", 2 * t + g)
                    for i in (0, 1):
                        name = f"C{i}"
                        B.wait_full(dve, name, f"L{g}", t)
                        B.free(dve.scalar_tensor_tensor(V["L"][:, i:4:2, :], split(bank[name][:, 0:2 * KEYS], 2),
                                                        HD ** -0.5, V["bias_v"][:, 4 * g + i:4 * g + 4:2, :],
                                                        ALU.mult, ALU.add), name)
                    g4 = slice(4 * g, 4 * g + 4)
                    dve.drain()
                    dve.tensor_reduce(V["negm"][:, g4], V["L"], AX.X, ALU.max)
                    dve.drain()
                    dve.tensor_tensor(V["negm"][:, g4], V["negm"][:, g4], row("sinks")[:, g4], ALU.max)
                    dve.drain()
                    dve.tensor_tensor(V["sd"][:, g4], row("sinks")[:, g4], V["negm"][:, g4], ALU.subtract)
                    dve.drain()
                    dve.tensor_scalar(V["negm"][:, g4], V["negm"][:, g4], -1.0, None, ALU.mult).then_inc(S["negm"], 1)
                    if g == 1 and isinstance(t, int) and t == 0:
                        dve.tensor_copy(V["bias_v"][0:64, :, 0:64], V["bias_first"][0:64])
                return go

            def att4(g):
                def go(t, b):
                    B.wait_full(dve, "T1", f"P{g}", t)
                    S.wait(dve, "pv", 2 * t + g)
                    B.free(dve.tensor_copy(V["PT"][:, 2:4, :], split(bank["T1"][:, :], 2)), "T1")
                return go

            def att5(t, b):
                S.wait(dve, "probs", 2 * t + 2)
                dve.tensor_tensor(V["den"], V["sm"], V["es"], ALU.add)
                dve.drain()
                dve.reciprocal(V["den"], V["den"])
                dve.drain()
                S.wait(dve, "pv", 2 * t + 2)
                dve.tensor_tensor(split(pk["ya"], QH), split(bank["C2"][:, :], QH), per_channel(V["den"], HD), ALU.mult).then_inc(S["ya"], 1)

            norm(0, 0)
            run(dve, {"norm": norm, "ev_r": ev("r"), "ev_k": ev("k"), "ev_v": ev("v"), "ev_lora": ev("lora"),
                      "att1": att1, "kk": kk, "ew1": ew1, "ew2": ew2, "ew3": ew3, "tok1": tok("tokB"), "tok2": tok("tokV"),
                      "att3_0": att3(0), "att3_1": att3(1), "att4_0": att4(0), "att4_1": att4(1), "att5_1": att5})


def views(nc, ctx):
    total = 53200
    arena = ctx.enter_context(nc.sbuf_tensor("arena", [P, total], F32))
    V = {}
    a = Arena(arena)
    for name, w in (("consts", NCONST), ("cols", NCOLS), ("rows", NROWS)):
        V[name] = a.take(w)
    V["k"] = lambda n: V["consts"][:, CONSTS[n][0]:CONSTS[n][1]]
    V["col"] = lambda n: V["cols"][:, COLS[n][0]:COLS[n][1]]
    V["row"] = lambda n: V["rows"][:, ROWS[n][0]:ROWS[n][1]]
    for name in ("s1", "b1", "s2", "b2"):
        V[name] = a.take(KD)
    V["omka"] = a.take(CC)
    V["minus_half"] = a.take(10)
    V["S"] = a.take(CC * HD)
    for name, w in (("idx", 2 * NT), ("top_w", 2 * NT)):
        V[name] = a.take(w)
    V["base_end"] = a.at

    V["bias"] = a.take(QH * KEYS)
    V["bias_v"] = split(V["bias"], QH)
    V["bias_first"] = split(a.take(QH * 64), QH)
    V["rksel"] = split(a.take(2 * CC), CC)
    V["w2"], V["g2"] = a.take(C), a.take(C)
    w_in_at = a.at
    V["w_in"] = split(a.take(KD * IN_COLS), KD)
    V["w_in_at"] = (w_in_at, a.at)
    for name, w in (("raw", NF * (P + 1)), ("qkv0", 768), ("qkv1", 768), ("Pb", 8 * 65), ("kT", 2 * KEYS), ("Pm", 1024)):
        V[name] = a.take(w)
    V["raw_v"], V["kT_v"], V["Pm_v"] = split(V["raw"], NF), split(V["kT"], 2), split(V["Pm"], 4)
    V["Pb_v"] = split(V["Pb"], 8)
    V["qkv"] = [V["qkv0"], V["qkv1"]]
    tail = a.at
    for name, w in (("x", D), ("junk", D), ("hT", D), ("ssx", 1), ("msx", 1), ("rsx", 1), ("delta", C), ("f0", NF * P),
                    ("f1", NF * P), ("tw", P), ("sg", P), ("sw", C), ("sa", C), ("kk", C), ("sq", C), ("ssm", 8),
                    ("ninv", 8), ("nT", P), ("cum", C), ("Pinv", C), ("kp", C),
                    ("ms10", 10), ("rs10", 10), ("qn", C + 256), ("kn", P), ("qT", C), ("L", 4 * KEYS), ("negm", 8),
                    ("sd", 8), ("sm", 8), ("es", 8), ("den", 8), ("PT", 1024), ("pk_all", NPK)):
        V[name] = a.take(w)
    V["hT"] = split(V["hT"], KD)
    V["sqk"], V["bb"], V["rk"] = V["junk"][:, 0:640], V["sw"], V["sq"]
    V["f"] = [split(V["f0"], NF), split(V["f1"], NF)]
    V["delta"], V["L"], V["PT"] = split(V["delta"], 4), split(V["L"], 4), split(V["PT"], 4)
    V["pk"] = {n: V["pk_all"][:, lo:hi] for n, (lo, hi) in PK.items()}
    V["pk"]["AR_v"] = V["pk"]["AR"].rearrange("p (c e n) -> p c e n", c=CC, e=2)
    assert a.at <= total, a.at

    s = Arena(arena, tail)
    V["ada_slots"] = [split(s.take(KD * 512), KD) for _ in range(2)]
    for name, w in (("csig", KD), ("cs", KD), ("cs_rows", KD * P), ("gt", 2 * D), ("onehot", 2 * CHUNK * CHUNK),
                    ("rel_bias", QH), ("mod0", 512), ("mod1", 512)):
        V[name] = s.take(w)
    assert s.at <= total, s.at
    V["cs_rows"] = split(V["cs_rows"], KD)
    V["mod"] = [V["mod0"], V["mod1"]]
    V["bias_sb"] = V["onehot"]
    return V, arena, total


_LV = range(1, len(LEVELS))
USES2 = {"Z0": ("M0", "M4", *(f"z{l}" for l in _LV), "G", "U0", "U1"),
         "Z1": ("M1", "M5", *(f"z{l}" for l in _LV), "I", "U0", "U1"),
         "X0": ("M2", "M6", "t0", *[f"{k}{l}" for l in _LV for k in "xt"][:-1], "WT"),
         "X1": ("M3", "M7", "t0", *[f"{k}{l}" for l in _LV for k in "xt"][:-1], "D0", "D1"),
         "YE": ("y",), "YO": ("y",),
         "O0": ("yT", "o", "hT", "rl"), "O1": ("yT", "o", "hT")}
BANK2 = {b: i for i, b in enumerate(("O0", "O1", "Z0", "Z1", "X0", "X1", "YE", "YO"))}


def views2(V, arena, total):
    a = Arena(arena, V["base_end"])
    for name, w in (("w_out", KD * D), ("w_router", KD * NR), ("gt1", D), ("pk0", NPK), ("pk1", NPK), ("MT", 4 * P * H),
                    ("X", P * H), ("XT", P * H), ("Z", P * H), ("ET0", P * H), ("ET1", P * H), ("G", C), ("U0", C),
                    ("WT", C), ("U", C), ("Stmp", C // 2), ("mu", 8), ("var", 8), ("rsy", 8), ("yc", C), ("sqy", C),
                    ("vb", C), ("yT", D), ("tmp", D), ("x1", D), ("xn2", D), ("h2T", D), ("junk2", D), ("ss2", 1),
                    ("ms2", 1), ("rs2", 1), ("g8", 8), ("m8", 8), ("i8", 8), ("gid", 1), ("ngm", 1), ("ge", 4), ("gs", 1),
                    ("ex", NE), ("eq", NE), ("off", NE), ("e8", 8), ("ei8", 8), ("dd", 1), ("de", 1), ("w0_", 1)):
        V["2" + name] = a.take(w)
    assert a.at <= total, a.at
    W = {n[1:]: v for n, v in V.items() if n[0] == "2"}
    for n in ("w_out", "w_router", "yT", "h2T"):
        W[n] = split(W[n], KD)
    for n in ("MT", "X", "XT", "Z", "ET0", "ET1"):
        W[n] = split(W[n], H)
    W["ET"] = [W["ET0"], W["ET1"]]
    W["pk"] = []
    for b in range(2):
        pk = {n: W[f"pk{b}"][:, lo:hi] for n, (lo, hi) in PK.items()}
        pk["AR"] = pk["AR"].rearrange("p (c e n) -> p c e n", c=CC, e=2)
        W["pk"].append(pk)
    for n in ("i8", "ei8"):
        W[n] = W[n].bitcast(U32)
    return W


def pass2(nc, S, ps, V, W, ins, dram, nt):
    B = Banks(S, "b", USES2, nt, ahead=sum((USES2[b] for b in ("Z0", "Z1", "X0", "X1", "YE")), ()))
    bank = {b: ps[i] for b, i in BANK2.items()}
    k, row = V["k"], V["row"]
    ident, level = k("ident"), split(k("level"), len(LEVELS))
    MT, X, XT, Z, ET = W["MT"], W["X"], W["XT"], W["Z"], W["ET"]
    St = split(V["S"], CC)
    half = lambda h: (64 * (h % 2), h // 2)
    hs = lambda h: slice(HD * h, HD * h + HD)
    by_head = lambda ap: ap.rearrange("p (c e n) -> p c e n", c=CC, e=2)
    M_BANKS = ("Z0", "Z1", "X0", "X1")
    last = len(LEVELS) - 1

    ORDER = (("Z2", 1), ("X2", 1), ("gn1", 0), ("T2", 1), ("h2T", -1), ("h2", -1), ("gn2", 0), ("Z3", 1), ("X3", 1),
             ("route", -1), ("yT", 0), ("load", 2), ("T3", 1), ("o0", 0), ("Z4", 1), ("o1", 0), ("pick", -1),
             ("X4", 1), ("o2", 0), ("weigh", -1), ("T4", 1), ("o3", 0), ("o4", 0), ("Z5", 1), ("o5", 0), ("X5", 1),
             ("o6", 0), ("o7", 0), ("W", 1), ("res0", 0), ("S0a", 1), ("o8", 0), ("o9", 0), ("S0b", 1), ("o10", 0),
             ("o11", 0), ("S1a", 1), ("o12", 0), ("S1b", 1), ("mean", 1), ("Ma", 2), ("o13", 0), ("Mb", 2),
             ("o14", 0), ("o15", 0), ("x2", 2), ("res1", 0), ("Z1", 2), ("var", 1), ("X1", 2), ("T1", 2), ("ss2", 0),
             ("norm2", 0))

    def run(eng, steps):
        def tile(t, parity, lo=-1, hi=2):
            for name, ahead in ORDER:
                if lo <= ahead <= hi and name in steps:
                    steps[name](t + ahead, (parity + ahead) % 2)

        tile(-2, 0, lo=2)
        tile(-1, 1, lo=1)
        tile(0, 0, lo=0)
        tile(1, 1)
        if nt > 4:
            with eng.Fori(1, nt // 2 - 1) as u:
                tile(2 * u, 0)
                tile(2 * u + 1, 1)
        tile(nt - 2, 0, hi=1)
        tile(nt - 1, 1, hi=0)
        tile(nt, 0, hi=-1)

    with nc.Block() as block:
        @block.sync
        def _(sp):
            def load(n, b):
                B.wait_full(sp, "O0", "yT", n - 2)
                if not isinstance(n, int) or n >= 2:
                    load_pack(sp, S, W, dram, n, b)
                if isinstance(n, int) and n == 0:
                    sp.dma_start(W["w_out"], ins["w_out"].rearrange("(k p) n -> p k n", p=P)).then_inc(S["w_out"], 16)
                fill = NB - FULL_BLOCKS
                if nt == NT:
                    for i in range(fill // NT):
                        sp.dma_start(dram["y"][bass.ds((n * (fill // NT) + FULL_BLOCKS + i) * P, P), :],
                                     V["consts"][:, 0:D]).then_inc(S["y_fill"], 16)

            def residual(t, b):
                S.wait(sp, "x1_out", 16 * t)
                S.wait(sp, "xn2", t)
                sp.dma_start(W["x1"], dram["x"][bass.ds(t * P, P), :]).then_inc(S["xres"], 16)

            def store_x1(t, b):
                S.wait(sp, "x1", t + 1)
                sp.dma_start(dram["x1"][bass.ds(t * P, P), :], W["x1"]).then_inc(S["x1_out"], 16)

            def store_xn2(t, b):
                S.wait(sp, "xn2", t + 1)
                sp.dma_start(dram["xn2"][bass.ds(t * P, P), :], W["xn2"]).then_inc(S["xn2_out"], 16)

            run(sp, {"load": load, "yT": residual, "res1": store_x1, "norm2": store_xn2})
            sp.wait_ge(S["xn2_out"], 16 * nt)
            sp.wait_ge(S["x1_out"], 16 * nt)
            if nt == NT:
                sp.wait_ge(S["y_fill"], 16 * (NB - FULL_BLOCKS))

        @block.tensor
        def _(pe):
            def wait_pack(n, b):
                S.wait(pe, f"pack{b}", 16 * (n // 2) + 16 if isinstance(n, int) else 8 * (n - b) + 16)

            def M(g):
                def go(n, b):
                    wait_pack(n, b)
                    pk = W["pk"][b]
                    for h in range(4 * g, 4 * g + 4):
                        hp, c = half(h)
                        name = M_BANKS[h % 4]
                        B.wait_free(pe, name, f"M{h}", n)
                        ar = pk["AR"][hp:hp + 64, c, :, :].rearrange("p e n -> p (e n)")
                        for i, f in enumerate(("BT", "KT")):
                            mm = pe.matmul(bank[name][:, 256 * i:256 * i + 256], pk[f][hp:hp + 64, P * c:P * c + P], ar,
                                           start=True, stop=True)
                        B.full(mm, name)
                return go

            def turn(n, use, wait):
                for g in range(2):
                    wait(g)
                    B.wait_free(pe, f"X{g}", use, n)
                    for i in range(4):
                        src = XT if use == "t0" else X
                        mm = pe.transpose(bank[f"X{g}"][:, P * i:P * i + P], src[:, 4 * g + i, :], ident)
                    B.full(mm, f"X{g}")

            def x2(n, b):
                turn(n, "t0", lambda g: S.wait(pe, "xt2", 2 * n + g + 1))

            def Zl(l):
                def go(n, b):
                    if l > 1:
                        S.wait(pe, "et", 4 * n + l - 1)
                    for g in range(2):
                        if l == 1:
                            S.wait(pe, "et1", 2 * n + g + 1)
                        B.wait_read(pe, f"X{g}", f"t{l - 1}", n)
                        B.wait_free(pe, f"Z{g}", f"z{l}", n)
                        for i in range(4):
                            h = 4 * g + i
                            mm = pe.matmul(bank[f"Z{g}"][:, P * i:P * i + P], ET[l % 2][:, h, :], X[:, h, :],
                                           start=True, stop=True)
                        B.full(mm, f"Z{g}")
                return go

            def Xl(l):
                def go(n, b):
                    for g in range(2):
                        B.wait_read(pe, f"Z{g}", f"z{l}", n)
                        B.wait_free(pe, f"X{g}", f"x{l}", n)
                        for i in range(4):
                            h = 4 * g + i
                            a, c = (Z, XT) if l == last else (XT, Z)
                            mm = pe.matmul(bank[f"X{g}"][:, P * i:P * i + P], a[:, h, :], c[:, h, :],
                                           start=True, stop=True)
                        B.full(mm, f"X{g}")
                return go

            def Tl(l):
                return lambda n, b: turn(n, f"t{l}", lambda g: B.wait_read(pe, f"X{g}", f"x{l}", n))

            def Wstep(n, b):
                pk = W["pk"][b]
                B.wait_free(pe, "Z0", "G", n)
                for h in range(H):
                    mm = pe.matmul(bank["Z0"][:, hs(h)], MT[:, h, 256:384], pk["V"][:, hs(h)], start=True, stop=True)
                B.full(mm, "Z0")
                for g in range(2):
                    B.wait_read(pe, f"X{g}", f"x{last}", n)
                B.wait_free(pe, "X0", "WT", n)
                for h in range(H):
                    hp, c = half(h)
                    mm = pe.matmul(bank["X0"][hp:hp + 64, P * c:P * c + P], pk["A"][:, hs(h)], XT[:, h, :],
                                   start=True, stop=True)
                B.full(mm, "X0")
                B.wait_read(pe, "Z0", "G", n)
                B.wait_free(pe, "Z1", "I", n)
                for h in range(H):
                    mm = pe.matmul(bank["Z1"][:, hs(h)], XT[:, h, :], W["G"][:, hs(h)], start=True, stop=True)
                B.full(mm, "Z1")

            def scan(q, part):
                rows = slice(64 * q, 64 * q + 64)

                def products(n, b):
                    pk = W["pk"][b]
                    if q == 0:
                        for e, name in enumerate(("YE", "YO")):
                            B.wait_free(pe, name, "y", n)
                            for c in range(CC):
                                h = 2 * c + e
                                pe.matmul(bank[name][:, hs(c)], MT[:, h, 384:512], pk["V"][:, hs(h)],
                                          start=(c == 0), stop=False, skip_group_check=True)
                        B.wait_read(pe, "X0", "WT", n)
                    S.wait(pe, "state", 2 * n + q)
                    for e, name in enumerate(("Z0", "Z1")):
                        B.wait_free(pe, name, f"U{q}", n)
                        pe.sem_inc(S["pe_passed"], 1)
                        for c in range(CC):
                            hp = 64 * e
                            mm = pe.matmul(bank[name][rows, hs(c)], W["WT"][hp:hp + 64, P * c + 64 * q:P * c + 64 * q + 64],
                                           St[hp:hp + 64, c, :], start=True, stop=True)
                        B.full(mm, name)
                    for e, name in enumerate(("YE", "YO")):
                        for c in range(CC):
                            hp = 64 * e
                            pe.matmul(bank[name][rows, hs(c)], pk["AR"][hp:hp + 64, c, 1, rows],
                                      St[hp:hp + 64, c, :], start=False, stop=False, skip_group_check=True)

                def update(n, b):
                    pk = W["pk"][b]
                    B.wait_free(pe, "X1", f"D{q}", n)
                    for e in range(2):
                        B.wait_read(pe, f"Z{e}", f"U{q}", n)
                    pe.sem_inc(S["pe_passed"], 1)
                    for h in range(H):
                        hp, c = half(h)
                        for i, (f, rhs) in enumerate((("B", W["U"]), ("K", pk["V"]))):
                            mm = pe.matmul(bank["X1"][hp:hp + 64, hs(c)], pk[f][rows, hs(h)], rhs[rows, hs(h)],
                                           start=(i == 0), stop=(i == 1))
                    B.full(mm, "X1")
                    if q == 1:
                        for e, name in enumerate(("YE", "YO")):
                            for c in range(CC):
                                h = 2 * c + e
                                mm = pe.matmul(bank[name][:, hs(c)], MT[:, h, 128:256], W["U"][:, hs(h)],
                                               start=False, stop=(c == CC - 1), skip_group_check=True)
                            B.full(mm, name)
                return (products, update)[part]

            def yT(t, b):
                pk = W["pk"][b]
                for name, src in (("O1", pk["ya"]), ("O0", W["yc"])):
                    B.wait_free(pe, name, "yT", t)
                    if name == "O0":
                        S.wait(pe, "yr", t + 1)
                    for c in range(CC):
                        mm = pe.transpose(bank[name][:, P * c:P * c + P], src[:, P * c:P * c + P], ident)
                    B.full(mm, name)

            def o(n0, kk):
                def go(t, b):
                    name = f"O{n0}"
                    if kk == 0:
                        if isinstance(t, int) and t == 0 and n0 == 0:
                            pe.wait_ge(S["w_out"], 48)
                        for other in ("O0", "O1"):
                            B.wait_read(pe, other, "yT", t)
                    mm = pe.matmul(bank[name][:, :], W["yT"][:, kk, :], W["w_out"][:, kk, 512 * n0:512 * n0 + 512],
                                   start=(kk == 0), stop=(kk == KD - 1))
                    if kk == KD - 1:
                        B.full(mm, name)
                return go

            def h2T(t, b):
                S.wait(pe, "xn2", t + 1)
                for g in range(2):
                    B.wait_free(pe, f"O{g}", "hT", t)
                    for i in range(4):
                        c = 4 * g + i
                        mm = pe.transpose(bank[f"O{g}"][:, P * i:P * i + P], W["xn2"][:, P * c:P * c + P], ident)
                    B.full(mm, f"O{g}")

            def route(t, b):
                B.wait_read(pe, "O1", "hT", t)
                B.wait_free(pe, "O0", "rl", t)
                for kk in range(KD):
                    mm = pe.matmul(bank["O0"][:, 0:NR], W["h2T"][:, kk, :], W["w_router"][:, kk, :],
                                   start=(kk == 0), stop=(kk == KD - 1))
                B.full(mm, "O0")

            run(pe, {"Ma": M(0), "Mb": M(1), "x2": x2, **{f"Z{l}": Zl(l) for l in _LV}, **{f"X{l}": Xl(l) for l in _LV},
                     **{f"T{l}": Tl(l) for l in range(1, last)}, "W": Wstep,
                     **{f"S{q}{'ab'[part]}": scan(q, part) for q in range(2) for part in range(2)}, "yT": yT,
                     **{f"o{8 * n0 + kk}": o(n0, kk) for n0 in range(2) for kk in range(KD)}, "h2T": h2T,
                     "route": route})

        @block.scalar
        def _(act):
            def turned(n, use, dst):
                for g in range(2):
                    B.wait_full(act, f"X{g}", use, n)
                    B.free(act.activation(dst[:, 4 * g:4 * g + 4, :], split(bank[f"X{g}"][:, :], 4), ACT.Copy), f"X{g}")

            def x2(n, b):
                turned(n, "t0", X)

            def Zl(l):
                def go(n, b):
                    for g in range(2):
                        B.wait_full(act, f"Z{g}", f"z{l}", n)
                        B.free(act.activation(Z[:, 4 * g:4 * g + 4, :], split(bank[f"Z{g}"][:, :], 4), ACT.Copy), f"Z{g}")
                return go

            def Tl(l):
                return lambda n, b: turned(n, f"t{l}", XT)

            def Wstep(n, b):
                for name, use, dst in (("Z0", "G", "G"), ("X0", "WT", "WT")):
                    B.wait_full(act, name, use, n)
                    B.free(act.activation(W[dst], bank[name][:, :], ACT.Copy), name)

            def nrm(t, b):
                S.wait(act, "yc", t + 1)
                act.activation(W["sqy"], W["yc"], ACT.Square).then_inc(S["sqy"], 1)

            def yT(t, b):
                for i, name in ((1, "O1"), (0, "O0")):
                    B.wait_full(act, name, "yT", t)
                    B.free(act.activation(W["yT"][:, 4 * i:4 * i + 4, :], split(bank[name][:, :], 4), ACT.Copy), name)

            def norm2(t, b):
                S.wait(act, "x1", t + 1)
                act.activation(W["junk2"], W["x1"], ACT.Square, accum_out=W["ss2"]).then_inc(S["ss2"], 1)

            def h2T(t, b):
                B.wait_full(act, "O0", "hT", t)
                for c in range(4):
                    a = act.activation(W["h2T"][:, c, :], bank["O0"][:, P * c:P * c + P], ACT.Identity,
                                       scale=V["s2"][:, c:c + 1], bias=V["b2"][:, c:c + 1])
                B.free(a, "O0")

            def pick(t, b):
                S.wait(act, "ngm", t + 1)
                act.activation(W["ge"], W["g8"][:, 0:NG], ACT.Exp, bias=W["ngm"][:, 0:1], accum_out=W["gs"])

            def weigh(t, b):
                S.wait(act, "dd", t + 1)
                act.activation(W["de"], W["dd"], ACT.Exp).then_inc(S["de"], 1)

            run(act, {"x2": x2, **{f"Z{l}": Zl(l) for l in _LV}, **{f"T{l}": Tl(l) for l in range(1, last)}, "W": Wstep,
                      "mean": nrm, "yT": yT, "ss2": norm2, "h2": h2T, "pick": pick, "weigh": weigh})

        @block.gpsimd
        def _(pool):
            def et(l):
                def go(n, b):
                    if l > 2:
                        B.wait_full(pool, "Z1", f"z{l - 2}", n)
                    pool.tensor_tensor(ET[l % 2], MT[:, :, 0:P], level[:, l:l + 1, :].to_broadcast([P, H, P]),
                                       ALU.mult).then_inc(S["et"], 1)
                return go

            def M(g):
                def go(n, b):
                    B.wait_read(pool, "X1", f"M{4 * g + 3}", n)
                    hd = slice(4 * g, 4 * g + 4)
                    pool.tensor_tensor(ET[1][:, hd, :], MT[:, hd, 0:P], level[:, 1:2, :].to_broadcast([P, 4, P]),
                                       ALU.mult).then_inc(S["et1"], 1)
                return go

            def var(t, b):
                S.wait(pool, "vary", t + 1)
                pool.tensor_tensor(W["rsy"], W["var"], V["minus_half"][:, 0:8], ALU.pow).then_inc(S["rsy"], 1)

            def gn1(t, b):
                B.wait_full(pool, "O1", "yT", t - 1)
                pool.tensor_tensor(split(W["vb"], H), split(W["pk"][b]["V"], H), per_channel(W["pk"][b]["bon"], HD),
                                   ALU.mult).then_inc(S["vb"], 1)

            def norm2(t, b):
                S.wait(pool, "ms2", t + 1)
                pool.tensor_tensor(W["rs2"], W["ms2"], V["minus_half"][:, 0:1], ALU.pow).then_inc(S["rs2"], 1)

            pool.memset(W["g8"], NEG).then_inc(S["g8_fill"], 1)
            run(pool, {"Ma": M(0), "Mb": M(1), **{f"Z{l - 2}": et(l) for l in _LV if l > 2}, "var": var, "gn1": gn1,
                       "ss2": norm2, "x2": et(2)})

        @block.vector
        def _(dve):
            def M(g):
                def go(n, b):
                    for h in range(4 * g, 4 * g + 4):
                        name = M_BANKS[h % 4]
                        B.wait_full(dve, name, f"M{h}", n)
                        B.free(dve.tensor_tensor(MT[:, h, :], bank[name][:, :], k("mmask"), ALU.mult), name)
                    dve.drain()
                    hd = slice(4 * g, 4 * g + 4)
                    dve.tensor_tensor(XT[:, hd, :], MT[:, hd, 0:P], level[:, 0:1, :].to_broadcast([P, 4, P]), ALU.mult)
                    dve.drain()
                    dve.tensor_tensor(XT[:, hd, :], XT[:, hd, :], ident.unsqueeze(1).to_broadcast([P, 4, P]),
                                      ALU.add).then_inc(S["xt2"], 1)
                return go

            def lvl(l):
                dst = XT if l == last else X

                def go(n, b):
                    for g in range(2):
                        B.wait_full(dve, f"X{g}", f"x{l}", n)
                        d = dst[:, 4 * g:4 * g + 4, :]
                        B.free(dve.tensor_tensor(d, d, split(bank[f"X{g}"][:, :], 4), ALU.add), f"X{g}")
                return go

            def Wstep(n, b):
                B.wait_full(dve, "Z1", "I", n)
                B.free(dve.tensor_copy(W["U0"], bank["Z1"][:, :]), "Z1")

            def scan(q):
                rows = slice(64 * q, 64 * q + 64)

                def go(n, b):
                    if q == 0:
                        dve.drain()
                    for e in range(2):
                        B.wait_full(dve, f"Z{e}", f"U{q}", n)
                        B.free(dve.tensor_tensor(by_head(W["U"])[rows, :, e, :], split(bank[f"Z{e}"][rows, 0:256], CC),
                                                 by_head(W["U0"])[rows, :, e, :], ALU.add), f"Z{e}")
                    B.wait_full(dve, "X1", f"D{q}", n)
                    B.free(dve.tensor_tensor(W["Stmp"], V["S"], bank["X1"][:, 0:256], ALU.add), "X1")
                    dve.drain()
                    pc = W["pk"][b]["PC"].rearrange("p (c q) -> p c q", q=2)[:, :, q:q + 1].to_broadcast([P, CC, HD])
                    dve.tensor_tensor(St, split(W["Stmp"], CC), pc, ALU.mult).then_inc(S["state"], 1)
                return go

            def mean(t, b):
                mu = W["mu"].rearrange("p (c e) -> p c e", e=2)
                yc = by_head(W["yc"])
                for e, name in enumerate(("YE", "YO")):
                    B.wait_full(dve, name, "y", t)
                    dve.tensor_reduce(mu[:, :, e:e + 1], split(bank[name][:, 0:256], CC), AX.X, ALU.add)
                dve.drain()
                dve.tensor_scalar(W["mu"], W["mu"], 1.0 / HD, None, ALU.mult)
                dve.drain()
                B.wait_full(dve, "O0", "yT", t - 1)
                for e, name in enumerate(("YE", "YO")):
                    B.free(dve.tensor_tensor(yc[:, :, e, :], split(bank[name][:, 0:256], CC),
                                             mu[:, :, e:e + 1].to_broadcast([P, CC, HD]), ALU.subtract), name)
                dve.engine_nop().then_inc(S["yc"], 1)

            def var(t, b):
                S.wait(dve, "sqy", t + 1)
                dve.tensor_reduce(W["var"], split(W["sqy"], H), AX.X, ALU.add)
                dve.drain()
                dve.tensor_scalar(W["var"], W["var"], 1.0 / HD, 64e-5, ALU.mult, ALU.add).then_inc(S["vary"], 1)

            def gn1(t, b):
                S.wait(dve, "rsy", t + 1)
                dve.tensor_tensor(split(W["yc"], H), split(W["yc"], H), per_channel(W["rsy"], HD), ALU.mult)
                dve.drain()
                dve.tensor_tensor(W["yc"], W["yc"], row("ln_w"), ALU.mult)
                dve.drain()
                dve.tensor_tensor(W["yc"], W["yc"], row("ln_b"), ALU.add)

            def gn2(t, b):
                dve.drain()
                S.wait(dve, "vb", t + 1)
                dve.tensor_tensor(W["yc"], W["yc"], W["vb"], ALU.add)
                dve.drain()
                dve.tensor_tensor(W["yc"], W["yc"], W["pk"][b]["gate"], ALU.mult).then_inc(S["yr"], 1)

            def res(n0):
                def go(t, b):
                    if isinstance(t, int) and t == 0 and n0 == 0:
                        dve.wait_ge(S["w_out"], 48)
                    S.wait(dve, "xres", 16 * t + 16)
                    cols = slice(512 * n0, 512 * n0 + 512)
                    B.wait_full(dve, f"O{n0}", "o", t)
                    B.free(dve.tensor_tensor(W["tmp"][:, cols], bank[f"O{n0}"][:, :], W["gt1"][:, cols], ALU.mult), f"O{n0}")
                    dve.drain()
                    i = dve.tensor_tensor(W["x1"][:, cols], W["x1"][:, cols], W["tmp"][:, cols], ALU.add)
                    if n0 == 1:
                        i.then_inc(S["x1"], 1)
                return go

            def h2T(t, b):
                B.wait_full(dve, "O1", "hT", t)
                for c in range(4, KD):
                    i = dve.tensor_scalar(W["h2T"][:, c, :], bank["O1"][:, P * (c - 4):P * (c - 4) + P],
                                          V["s2"][:, c:c + 1], V["b2"][:, c:c + 1], ALU.mult, ALU.add)
                B.free(i, "O1")

            def ss2(t, b):
                S.wait(dve, "ss2", t + 1)
                dve.tensor_scalar(W["ms2"], W["ss2"], 1.0 / D, 1e-6, ALU.mult, ALU.add).then_inc(S["ms2"], 1)

            def norm2(t, b):
                S.wait(dve, "rs2", t + 1)
                S.wait(dve, "xn2_out", 16 * t)
                B.wait_full(dve, "O1", "hT", t - 1)
                dve.tensor_scalar(W["xn2"], W["x1"], W["rs2"][:, 0:1], None, ALU.mult).then_inc(S["xn2"], 1)

            def route(t, b):
                rb = row("rb")
                S.wait(dve, "de", t)
                B.wait_full(dve, "O0", "rl", t)
                dve.tensor_tensor(W["g8"][:, 0:NG], bank["O0"][:, 0:NG], rb[:, 0:NG], ALU.add)
                B.free(dve.tensor_tensor(W["ex"], bank["O0"][:, NG:NR], rb[:, NG:NR], ALU.add), "O0")

            def pick(t, b):
                dve.drain()
                dve.max(W["m8"], W["g8"])
                dve.drain()
                dve.tensor_scalar(W["ngm"], W["m8"][:, 0:1], -1.0, None, ALU.mult).then_inc(S["ngm"], 1)
                dve.max_index(W["i8"], W["m8"], W["g8"])
                dve.drain()
                dve.tensor_copy(W["gid"], W["i8"][:, 0:1])
                dve.drain()
                dve.tensor_scalar(W["eq"], k("group_e"), W["gid"][:, 0:1], None, ALU.is_equal)
                dve.drain()
                dve.tensor_scalar(W["off"], W["eq"], 1.0, 1e30, ALU.subtract, ALU.mult)
                dve.tensor_tensor(W["ex"], W["ex"], W["eq"], ALU.mult)
                dve.drain()
                dve.tensor_tensor(W["ex"], W["ex"], W["off"], ALU.add)

            def weigh(t, b):
                dve.drain()
                dve.max(W["e8"], W["ex"])
                dve.drain()
                dve.tensor_tensor(W["dd"], W["e8"][:, 1:2], W["e8"][:, 0:1], ALU.subtract).then_inc(S["dd"], 1)
                dve.max_index(W["ei8"], W["e8"], W["ex"])
                dve.drain()
                dve.tensor_copy(V["idx"][:, bass.ds(2 * t, 2)], W["ei8"][:, 0:2])
                S.wait(dve, "de", t + 1)
                dve.scalar_tensor_tensor(W["w0_"], W["de"], 1.0, W["gs"], ALU.add, ALU.mult)
                dve.drain()
                dve.reciprocal(W["w0_"], W["w0_"])
                dve.drain()
                dve.tensor_copy(V["top_w"][:, bass.ds(2 * t, 1)], W["w0_"])
                dve.tensor_tensor(V["top_w"][:, bass.ds(2 * t + 1, 1)], W["w0_"], W["de"], ALU.mult)

            dve.wait_ge(S["g8_fill"], 1)
            run(dve, {"Ma": M(0), "Mb": M(1), **{f"X{l}": lvl(l) for l in _LV}, "W": Wstep, "S0a": scan(0),
                      "S1a": scan(1), "mean": mean, "var": var, "gn1": gn1, "gn2": gn2, "res0": res(0), "res1": res(1), "ss2": ss2,
                      "norm2": norm2, "h2": h2T, "route": route, "pick": pick, "weigh": weigh})


SLOTS = 3
FLIGHT = 4
SLOT = 3 * KD * FE


def views3(V, arena, total):
    a = Arena(arena, V["base_end"])
    W = {}
    for name, w in (("slots", SLOTS * SLOT), ("gt2", D), ("xT", D), ("h", FE), ("hT", FE), ("xg", D), ("ysb", D),
                    ("sg", FE), ("dest", 2 * NT), ("row_tok", NB + 1), ("idx_now", 1), ("tab", 2 * NB + NE), ("nblk", 1)):
        W[name] = a.take(w)
    x1_at = V["base_end"] + (SLOTS - 1) * SLOT
    W["x1"] = arena[:, x1_at:x1_at + NT * D]
    assert NT * D <= SLOT + 3 * D + 2 * FE
    W["rows_of"] = [a.take(2).bitcast(U32) for _ in range(FLIGHT)]
    for name in ("dest", "idx_now"):
        W[name] = W[name].bitcast(U32)
    for name in ("row_tok", "tab", "nblk"):
        W[name] = W[name].bitcast(I32)
    at = a.at
    for name, w in (("oh0", NT * NE), ("oh1", NT * NE), ("ohs", NT * NE), ("pre", (NT + 1) * NE)):
        W[name] = a.take(w)
    for name in ("cnt", "nb", "nbi", "eb", "pend", "pstart"):
        W[name] = a.take(NE)
    for name in ("destf", "desti", "lo", "hi", "lof", "hif", "pos", "tokI"):
        W[name] = a.take(2 * NT)
    for name in ("be", "bei", "bef", "m3", "m3f"):
        W[name] = a.take(NB)
    assert a.at <= total, (a.at, at)
    W["cmp"] = arena[:, V["base_end"] + SLOTS * SLOT + D:V["base_end"] + SLOTS * SLOT + D + NB * NE]
    for name in ("nbi", "desti", "lo", "hi", "tokI", "bei", "m3"):
        W[name] = W[name].bitcast(I32)
    W["pos"] = W["pos"].bitcast(U32)
    return W


def dispatch(nc, S, ps, V, W, ins, dram):
    k = V["k"]
    te = lambda ap: ap.rearrange("p (t e) -> p t e", e=NE)
    idx = V["idx"].rearrange("p (t c) -> p t c", c=2)
    with nc.Block() as block:
        @block.sync
        def _(sp):
            sp.wait_ge(S["fill"], 1)
            sp.dma_start(dram["row_tok"].rearrange("(p b) o -> p (b o)", p=P), W["row_tok"]).then_inc(S["filled"], 16)
            sp.dma_start(W["gt2"], dram["gates"][:, D:2 * D]).then_inc(S["gt2"], 16)
            load_expert(sp, S, W, ins, 0, 0)
            sp.wait_ge(S["tok_rows"], 16 * 2 * NT)
            sp.dma_start(W["row_tok"], dram["row_tok"].rearrange("(p b) o -> p (b o)", p=P)).then_inc(S["filled"], 16)
            sp.wait_ge(S["filled"], 32)
            sp.wait_ge(S["gt2"], 16)

        @block.gpsimd
        def _(pool):
            pool.memset(W["row_tok"], T).then_inc(S["fill"], 1)
            pool.wait_ge(S["filled"], 16)
            pool.wait_ge(S["pos"], 1)
            for i in range(2 * NT):
                pool.indirect_dma_start(dram["row_tok"], bass.IndirectOffsetOnAxis(ap=W["pos"][:, i:i + 1], axis=0),
                                        W["tokI"][:, i:i + 1], None).then_inc(S["tok_rows"], 16)
            pool.wait_ge(S["tok_rows"], 16 * 2 * NT)

        @block.tensor
        def _(pe):
            pe.wait_ge(S["pre"], 1)
            pe.matmul(ps[0][:, :], k("before"), W["ohs"], start=True, stop=False)
            pe.matmul(ps[0][:, :], k("ones"), W["pre"][:, 0:NT * NE], start=False, stop=True)
            pe.matmul(ps[1][:, 0:NE], k("ones"), W["pre"][:, NT * NE:], start=True, stop=True).then_inc(S["rank"], 1)

        @block.vector
        def _(dve):
            def do(ins):
                dve.drain()

            iota = k("iota_e").unsqueeze(1).to_broadcast([P, NT, NE])
            for c in range(2):
                dve.tensor_tensor(te(W[f"oh{c}"]), iota, idx[:, :, c:c + 1].to_broadcast([P, NT, NE]), ALU.is_equal)
            dve.memset(W["pre"][:, 0:NE], 0.0)
            do(dve.tensor_copy(W["tokI"].rearrange("p (t c) -> p t c", c=2), per_channel(k("token"), 2)))
            do(dve.tensor_tensor(W["ohs"], W["oh0"], W["oh1"], ALU.add))
            for t in range(NT):
                a = slice(NE * t, NE * t + NE)
                i = dve.tensor_tensor(W["pre"][:, NE * t + NE:NE * t + 2 * NE], W["pre"][:, a], W["ohs"][:, a], ALU.add)
                if t == NT - 1:
                    i.then_inc(S["pre"], 1)
                else:
                    dve.drain()
            dve.wait_ge(S["rank"], 1)
            do(dve.tensor_scalar(W["cnt"], ps[1][:, 0:NE], float(P - 1), None, ALU.add))
            do(dve.tensor_copy(W["nbi"], W["cnt"]))
            do(dve.tensor_scalar(W["nbi"], W["nbi"], 7, None, ALU.arith_shift_right))
            do(dve.tensor_copy(W["nb"], W["nbi"]))
            do(dve.tensor_tensor_scan(W["eb"], k("ones")[:, 0:NE], W["nb"], 0.0, ALU.mult, ALU.add))
            dve.tensor_scalar(W["pend"], W["eb"], float(P), None, ALU.mult)
            do(dve.tensor_tensor(W["pstart"], W["eb"], W["nb"], ALU.subtract))
            do(dve.tensor_scalar(W["pstart"], W["pstart"], float(P), None, ALU.mult))
            do(dve.tensor_tensor(te(W["ohs"]), te(ps[0][:, :]), W["pstart"].unsqueeze(1).to_broadcast([P, NT, NE]), ALU.add))
            for c in range(2):
                dve.tensor_tensor(W[f"oh{c}"], W[f"oh{c}"], W["ohs"], ALU.mult)
            dve.drain()
            destf = W["destf"].rearrange("p (t c) -> p t c", c=2)
            for c in range(2):
                dve.tensor_reduce(destf[:, :, c:c + 1], te(W[f"oh{c}"]), AX.X, ALU.add)
            dve.drain()
            dve.tensor_copy(W["dest"], W["destf"])
            do(dve.tensor_copy(W["desti"], W["destf"]))
            dve.tensor_scalar(W["lo"], W["desti"], P - 1, None, ALU.bitwise_and)
            do(dve.tensor_scalar(W["hi"], W["desti"], 7, None, ALU.arith_shift_right))
            dve.tensor_copy(W["lof"], W["lo"])
            do(dve.tensor_copy(W["hif"], W["hi"]))
            do(dve.scalar_tensor_tensor(W["destf"], W["lof"], float(NB + 1), W["hif"], ALU.mult, ALU.add))
            dve.tensor_copy(W["pos"], W["destf"]).then_inc(S["pos"], 1)
            be3 = W["cmp"].rearrange("p (b e) -> p b e", e=NE)
            do(dve.tensor_tensor(be3, W["pend"].unsqueeze(1).to_broadcast([P, NB, NE]), per_channel(k("block_row"), NE),
                                 ALU.is_le))
            do(dve.tensor_reduce(W["be"], be3, AX.X, ALU.add))
            do(dve.tensor_scalar(W["be"], W["be"], float(NE - 1), None, ALU.min))
            do(dve.tensor_scalar(W["bef"], W["be"], 11.0, None, ALU.mult))
            do(dve.tensor_copy(W["bei"], W["bef"]))
            do(dve.tensor_scalar(W["m3"], W["bei"], 5, None, ALU.arith_shift_right))
            do(dve.tensor_copy(W["m3f"], W["m3"]))
            do(dve.scalar_tensor_tensor(W["m3f"], W["m3f"], -float(SLOTS), W["be"], ALU.mult, ALU.add))
            dve.tensor_scalar(W["tab"][:, 0:NB], W["m3f"], float(SLOT), None, ALU.mult)
            dve.tensor_scalar(W["tab"][:, NB:2 * NB], W["be"], 48.0, 48.0, ALU.mult, ALU.add)
            dve.tensor_scalar(W["tab"][:, 2 * NB:], W["eb"], 1.0, None, ALU.add)
            dve.tensor_copy(W["nblk"], W["eb"][:, NE - 1:NE])


def load_expert(eng, S, W, ins, e, slot):
    S.wait(eng, "weights", 48 * e)
    if not isinstance(e, int):
        eng.sem_inc(S["sp_passed"], 1)
    base = W["slots"][:, SLOT * slot:SLOT * slot + SLOT]
    for i, (name, rows) in enumerate((("w1", KD), ("w3", KD), ("w2e", FE // P))):
        src = ins[name][bass.ds(e, 1)].rearrange("a (k p) n -> p (a k) n", p=P)
        eng.dma_start(split(base[:, KD * FE * i:KD * FE * i + KD * FE], rows), src).then_inc(S["weights"], 16)


LAST_OF_SLOT = max(e for e in range(NE) if e % SLOTS == SLOTS - 1)
X1_EARLY = SLOT // D


def load_x1(eng, S, W, dram, t0, n):
    src = dram["x1"][t0 * P:(t0 + n) * P, :].rearrange("(t p) n -> p t n", p=P)
    eng.dma_start(split(W["x1"][:, D * t0:D * (t0 + n)], n), src).then_inc(S["x1_in"], 16)


def experts(nc, S, ps, V, W, ins, dram):
    ident = V["k"]("ident")
    bank = dict(zip(("HA", "HB", "HT", "X0", "X1", "Y0", "Y1"), ps))
    xT, hT, h = split(W["xT"], KD), split(W["hT"], FE // P), W["h"]
    with nc.Block() as block:
        @block.sync
        def _(sp):
            def load(e, slot):
                done = sp.value_load(W["tab"][0:1, bass.ds(2 * NB + e - SLOTS, 1)], min_val=1, max_val=NB + 1)
                sp.wait_ge(S["blocks_done"], done)
                sp.sem_inc(S["sp_passed"], 1)
                load_expert(sp, S, W, ins, e, slot)

            for e in range(1, SLOTS):
                load_expert(sp, S, W, ins, e, e)
            with sp.Fori(1, NE // SLOTS) as j:
                for i in range(SLOTS):
                    load(SLOTS * j + i, i)
            for e in range(NE // SLOTS * SLOTS, NE):
                load(e, e % SLOTS)
            done = sp.value_load(W["tab"][0:1, 2 * NB + LAST_OF_SLOT:2 * NB + LAST_OF_SLOT + 1], min_val=1,
                                 max_val=NB + 1)
            sp.wait_ge(S["blocks_done"], done)
            sp.sem_inc(S["sp_passed"], 1)
            for i in range(X1_EARLY // 3):
                load_x1(sp, S, W, dram, 3 * i, 3)
                sp.wait_ge(S["x1_in"], 16 * (i + 1))
            sp.wait_ge(S["weights"], 48 * NE)

        @block.gpsimd
        def _(pool):
            def gather(b):
                pool.tensor_copy(W["idx_now"].bitcast(I32), W["row_tok"][:, bass.ds(b, 1)])
                pool.drain()
                pool.indirect_dma_start(W["xg"], None, dram["xn2"],
                                        bass.IndirectOffsetOnAxis(ap=W["idx_now"], axis=0)).then_inc(S["xg"], 16)

            nblk = pool.value_load(W["nblk"][0:1, 0:1], min_val=1, max_val=NB)
            gather(0)
            with pool.Fori(0, NB) as b:
                with pool.If(b < nblk):
                    pool.wait_ge(S["x_turned"], b + 1)
                    gather(b + 1)

        @block.tensor
        def _(pe):
            def turn_x(b):
                pe.wait_ge(S["xg"], 16 * b + 16)
                for g in range(2):
                    for i in range(4):
                        c = 4 * g + i
                        mm = pe.transpose(bank[f"X{g}"][:, P * i:P * i + P], W["xg"][:, P * c:P * c + P], ident)
                mm.then_inc(S["x_turned"], 1)

            nblk = pe.value_load(W["nblk"][0:1, 0:1], min_val=1, max_val=NB)
            pe.sem_inc(S["blocks_done"], 1)
            turn_x(0)
            with pe.Fori(0, NB) as b:
                with pe.If(b < nblk):
                    slot = pe.value_load(W["tab"][0:1, bass.ds(b, 1)], min_val=0, max_val=(SLOTS - 1) * SLOT)
                    in_at = pe.value_load(W["tab"][0:1, bass.ds(b + NB, 1)], min_val=48, max_val=48 * NE)
                    w = lambda i, kk, n0, n: W["slots"][:, bass.ds(slot + KD * FE * i + kk + n0, n)]
                    pe.wait_ge(S["weights"], in_at)
                    pe.wait_ge(S["xT"], b + 1)
                    def up(g, i):
                        for kk in range(KD):
                            mm = pe.matmul(bank[("HA", "HB")[g]][:, 256 * i:256 * i + 256], xT[:, kk, :],
                                           w(i, FE * kk, 256 * g, 256), start=(kk == 0), stop=(kk == KD - 1))
                        if i == 1:
                            mm.then_inc(S["up"], 1)

                    def turn_h(g):
                        pe.wait_ge(S["h"], 2 * b + g + 1)
                        for c in (2 * g, 2 * g + 1):
                            mm = pe.transpose(bank["HT"][:, P * c:P * c + P], h[:, P * c:P * c + P], ident)
                        mm.then_inc(S["h_turned"], 1)

                    def down(g, n0):
                        for c in (2 * g, 2 * g + 1):
                            mm = pe.matmul(bank[f"Y{n0}"][:, :], hT[:, c, :], w(2, D * c, 512 * n0, 512),
                                           start=(c == 0), stop=(c == 3))
                        return mm

                    up(0, 0)
                    up(0, 1)
                    up(1, 0)
                    turn_h(0)
                    turn_x(b + 1)
                    up(1, 1)
                    pe.wait_ge(S["hT"], 2 * b + 1)
                    pe.wait_ge(S["y_read"], b + 1)
                    down(0, 0)
                    turn_h(1)
                    down(0, 1)
                    pe.wait_ge(S["hT"], 2 * b + 2)
                    down(1, 0)
                    mm = down(1, 1)
                    mm.then_inc(S["blocks_done"], 1)

        @block.scalar
        def _(act):
            def turned_x(b):
                act.wait_ge(S["x_turned"], b + 1)
                for c in range(KD):
                    a = act.activation(xT[:, c, :], bank[f"X{c // 4}"][:, P * (c % 4):P * (c % 4) + P], ACT.Identity,
                                       scale=V["s2"][:, c:c + 1], bias=V["b2"][:, c:c + 1])
                a.then_inc(S["xT"], 1)

            nblk = act.value_load(W["nblk"][0:1, 0:1], min_val=1, max_val=NB)
            act.sem_inc(S["y_out"], 16)
            turned_x(0)
            with act.Fori(0, NB) as b:
                with act.If(b < nblk):
                    for g, name in enumerate(("HA", "HB")):
                        act.wait_ge(S["up"], 2 * b + g + 1)
                        act.activation(W["sg"][:, 256 * g:256 * g + 256], bank[name][:, 0:256],
                                       ACT.Sigmoid).then_inc(S["sg"], 1)
                    turned_x(b + 1)
                    act.wait_ge(S["y_read"], b + 2)
                    act.sem_inc(S["act_passed"], 1)
                    act.dma_start(dram["y"][bass.ds(b * P, P), :], W["ysb"]).then_inc(S["y_out"], 16)
            act.wait_ge(S["y_out"], nblk * 16 + 16)
            act.sem_inc(S["act_passed"], 1)

        @block.vector
        def _(dve):
            nblk = dve.value_load(W["nblk"][0:1, 0:1], min_val=1, max_val=NB)
            dve.sem_inc(S["y_read"], 1)
            with dve.Fori(0, NB) as b:
                with dve.If(b < nblk):
                    for g, name in enumerate(("HA", "HB")):
                        cols = slice(256 * g, 256 * g + 256)
                        dve.wait_ge(S["sg"], 2 * b + g + 1)
                        dve.tensor_tensor(W["sg"][:, cols], W["sg"][:, cols], bank[name][:, 0:256], ALU.mult)
                        dve.drain()
                        dve.tensor_tensor(h[:, cols], W["sg"][:, cols], bank[name][:, 256:512], ALU.mult).then_inc(S["h"], 1)
                        dve.wait_ge(S["h_turned"], 2 * b + g + 1)
                        dve.tensor_copy(hT[:, 2 * g:2 * g + 2, :],
                                        split(bank["HT"][:, 256 * g:256 * g + 256], 2)).then_inc(S["hT"], 1)
                    dve.wait_ge(S["blocks_done"], b + 2)
                    dve.wait_ge(S["y_out"], b * 16 + 16)
                    for n0 in range(2):
                        cols = slice(512 * n0, 512 * n0 + 512)
                        i = dve.tensor_tensor(W["ysb"][:, cols], bank[f"Y{n0}"][:, :], W["gt2"][:, cols], ALU.mult)
                    i.then_inc(S["y_read"], 1)


def combine(nc, S, V, W, dram):
    buf = [{n: W["slots"][:, D * (4 * b + i):D * (4 * b + i) + D] for i, n in enumerate(("y0", "y1", "sum", "res"))}
           for b in range(FLIGHT)]

    def run(eng, step):
        for t in range(FLIGHT):
            step(t, t)
        with eng.Fori(1, NT // FLIGHT - 1) as u:
            for b in range(FLIGHT):
                step(FLIGHT * u + b, b)
        for t in range(NT - FLIGHT, NT):
            step(t, t % FLIGHT)

    with nc.Block() as block:
        @block.sync
        def _(sp):
            load_x1(sp, S, W, dram, X1_EARLY, NT - X1_EARLY)
            sp.wait_ge(S["x1_in"], 16 * (X1_EARLY // 3 + 1))

        @block.gpsimd
        def _(pool):
            def step(t, b):
                S.wait(pool, "summed", t - FLIGHT + 1)
                S.wait(pool, "rows_of", t + 1)
                pool.sem_inc(S["pool_passed"], 1)
                for c in range(2):
                    pool.indirect_dma_start(buf[b][f"y{c}"], None, dram["y"],
                                            bass.IndirectOffsetOnAxis(ap=W["rows_of"][b][:, c:c + 1],
                                                                      axis=0)).then_inc(S[f"y_in{b}"], 16)
            run(pool, step)

        @block.vector
        def _(dve):
            def rows_of(t, b):
                dve.tensor_copy(W["rows_of"][b], W["dest"][:, bass.ds(2 * t, 2)]).then_inc(S["rows_of"], 1)

            def step(t, b):
                m = buf[b]
                S.wait(dve, f"y_in{b}", 8 * (t - b) + 32)
                S.wait(dve, f"stored_out{b}", 4 * (t - b))
                dve.scalar_tensor_tensor(m["sum"], m["y0"], V["top_w"][:, bass.ds(2 * t, 1)],
                                         W["x1"][:, bass.ds(D * t, D)], ALU.mult, ALU.add)
                dve.drain()
                dve.scalar_tensor_tensor(m["res"], m["y1"], V["top_w"][:, bass.ds(2 * t + 1, 1)], m["sum"], ALU.mult,
                                         ALU.add).then_inc(S["summed"], 1)
                if not isinstance(t, int) or t < NT - FLIGHT:
                    rows_of(t + FLIGHT, b)

            for t in range(FLIGHT):
                rows_of(t, t)
            dve.wait_ge(S["x1_in"], 16 * (X1_EARLY // 3 + 1))
            run(dve, step)

        @block.scalar
        def _(act):
            def step(t, b):
                S.wait(act, "summed", t + 1)
                act.dma_start(dram["out"][bass.ds(t * P, P), :], buf[b]["res"]).then_inc(S[f"stored_out{b}"], 16)
            run(act, step)
            for b in range(FLIGHT):
                act.wait_ge(S[f"stored_out{b}"], 4 * NT)


def program(nc, ins, out, nt=NT, stages=9):
    with ExitStack() as ctx:
        S = Sync(nc, ctx)
        ps = [ctx.enter_context(nc.psum_tensor(f"ps{i}", [P, 512], F32)) for i in range(8)]
        V, arena, total = views(nc, ctx)
        scratch = lambda n, shape, dt=F32: nc.dram_tensor(n, shape, dt, kind="Internal").ap()
        dram = {"x": ins["x"], "gates": scratch("gates", [P, 2 * D]), "bias": scratch("bias", [QH, 2 * CHUNK * CHUNK]), "mid": scratch("mid", [NT, P, NPK]),
                "x1": scratch("x1", [T, D]), "xn2": scratch("xn2", [T + 1, D]),
                "row_tok": scratch("row_tok", [(NB + 1) * P, 1], I32), "y": scratch("y", [NB * P, D]), "out": out}
        setup(nc, S, ps, V, ins, dram)
        W = views2(V, arena, total)
        assert V["w_in_at"][0] <= V["base_end"] + KD * D and V["base_end"] + KD * (D + NR) + D + 2 * NPK <= V["w_in_at"][1]
        pass1(nc, S, ps, V, W, ins, dram, nt)
        pass2(nc, S, ps, V, W, ins, dram, nt)
        if stages < 3:
            return
        W = views3(V, arena, total)
        dispatch(nc, S, ps, V, W, ins, dram)
        experts(nc, S, ps, V, W, ins, dram)
        combine(nc, S, V, W, dram)


def host_arrays(inputs):
    a = {n: np.asarray(v) for n, v in inputs.items()}
    cols = np.zeros((P, NCOLS), np.float32)

    def col(name, v):
        v = v.reshape(-1)
        lo, hi = COLS[name]
        cols[:, lo:hi] = v.reshape(hi - lo, P).T

    mix = a["rwkv_shift_mix"].reshape(-1)
    col("mix", np.concatenate([mix[:3 * C + LORA_WA], np.zeros(P - LORA_WA, np.float32),
                               mix[3 * C + LORA_WA:], np.zeros(P - LORA_G, np.float32)]))
    for name, src in (("c", "c"), ("ada_b", "ada_b"), ("n1g", "norm1_g"), ("n2g", "norm2_g"), ("w0", "rwkv_w0"),
                      ("a0", "rwkv_a0"), ("k_k", "rwkv_k_k"), ("k_a", "rwkv_k_a"), ("r_k", "rwkv_r_k")):
        col(name, a[src])
    rows = np.concatenate([a[n].reshape(-1) for n in ("rwkv_ln_w", "rwkv_ln_b", "q_norm_g", "k_norm_g", "attn_sinks",
                                                      "router_grp_b", "router_exp_b")])[None, :]
    b = a["ada_b"].reshape(6, D)
    consts, onehot = shape_constants()
    return {"x": a["x"].reshape(T, D), "cols": cols, "rows": rows, "consts": consts, "onehot": onehot,
            "gate_b": np.concatenate([b[2], b[5]])[None, :],
            "ada_w": a["ada_w"][0], "w_in": a["w_in"][0], "w2": a["rwkv_w2"][0], "a2": a["rwkv_a2"][0],
            "g2": a["rwkv_g2"][0], "rel_bias": a["rel_bias"], "w_out": a["w_out"][0],
            "w_router": np.concatenate([a["router_grp_w"][0], a["router_exp_w"][0]], 1),
            "w1": a["exp_w1"][0], "w3": a["exp_w3"][0], "w2e": a["exp_w2"][0]}


def kernel(**inputs):
    import concourse.bacc as bacc
    from concourse.bass_utils import run_bass_kernel_spmd

    nc = bacc.Bacc("TRN2", target_bir_lowering=False, num_devices=1)
    arrays = {n: np.ascontiguousarray(v) for n, v in host_arrays(inputs).items()}
    ins = {n: nc.dram_tensor(n, v.shape, mybir.dt.from_np(v.dtype), kind="ExternalInput").ap() for n, v in arrays.items()}
    out = nc.dram_tensor("out", (T, D), F32, kind="ExternalOutput").ap()
    program(nc, ins, out)
    result = run_bass_kernel_spmd(nc, [arrays], core_ids=[0])
    return result.results[0]["out"].reshape(1, T, D)
```
